# Optimizing a Trainium2 kernel written in Bass

```python
import jax
import jax.numpy as jnp
from jax import lax
import numpy as np
import math
import jax, jax.numpy as jnp

D_MODEL = 1024
BATCH = 1
SEQ = 512
DEPTH = 1

GRID_W = 64
CTX_LEN = 256
EPS = 1e-6
N_MOD = 6

HG_HEADS = 8
HG_DK = 128
HG_DV = 128
HG_WIDTH = HG_HEADS * HG_DK
HG_CHUNK = 32

CONV_WIDTH = D_MODEL
CONV_K = 3

N_HEADS = 16
N_KV_HEADS = 4
HEAD_DIM = 64
GQA_GROUP = N_HEADS // N_KV_HEADS
ATTN_WIDTH = N_HEADS * HEAD_DIM
KV_WIDTH = N_KV_HEADS * HEAD_DIM
Q_BLOCK = 128
ROPE_THETA = 10000.0
ATTN_SCALE = HEAD_DIM ** -0.5

N_BRANCHES = 3
IN_SPLITS = (HG_WIDTH,) * 5 + (CONV_WIDTH,) * 3 + (ATTN_WIDTH, KV_WIDTH, KV_WIDTH) + (D_MODEL,) * N_BRANCHES
IN_WIDTH = 5 * HG_WIDTH + 3 * CONV_WIDTH + ATTN_WIDTH + 2 * KV_WIDTH + N_BRANCHES * D_MODEL

N_EXPERTS = 16
EXPERT_FF = 1024
CAPACITY_FACTOR = 2


def rmsnorm(x, g):
    xf = x.astype(jnp.float32)
    y = xf * lax.rsqrt(jnp.mean(xf * xf, axis=-1, keepdims=True) + EPS)
    return (y * g).astype(x.dtype)

def modulation(cvec, w, b):
    mod = jax.nn.silu(cvec) @ w + b
    return jnp.split(mod[:, None, :], N_MOD, axis=-1)

def modulate(h, g, shift, scale):
    return rmsnorm(h, g) * (1 + scale) + shift

def project(h, w_in):
    p = h @ w_in
    return jnp.split(p, np.cumsum(IN_SPLITS)[:-1].tolist(), axis=-1)

def to_heads(t, d):
    return t.reshape(t.shape[0], t.shape[1], -1, d)

def axial_rope_tables(n):
    rows = n // GRID_W
    row = jnp.repeat(jnp.arange(rows), GRID_W).astype(jnp.float32)
    col = jnp.tile(jnp.arange(GRID_W), rows).astype(jnp.float32)
    inv = ROPE_THETA ** (-jnp.arange(0, HEAD_DIM // 2, 2, dtype=jnp.float32) / (HEAD_DIM // 2))
    ang = jnp.concatenate([row[:, None] * inv, col[:, None] * inv], axis=-1)
    return jnp.cos(ang), jnp.sin(ang)

def apply_rope(x, cos, sin):
    x1, x2 = x[..., 0::2], x[..., 1::2]
    c, s = cos[None, :, None, :], sin[None, :, None, :]
    return jnp.stack([x1 * c - x2 * s, x1 * s + x2 * c], axis=-1).reshape(x.shape).astype(x.dtype)

def hgrn_chunk_scan(q, log_f, k, v, s0):
    bsz, n, h, _ = q.shape
    dv = v.shape[-1]
    nc = n // HG_CHUNK

    def chunks(t):
        return t.astype(jnp.float32).reshape(bsz, nc, HG_CHUNK, h, t.shape[-1]).transpose(1, 0, 3, 2, 4)

    lower = jnp.tril(jnp.ones((HG_CHUNK, HG_CHUNK), dtype=bool))[:, :, None]

    def step(s, blk):
        qc, lfc, kc, vc = blk
        b = jnp.cumsum(lfc, axis=2)
        decay = jnp.exp(jnp.where(lower, b[:, :, :, None, :] - b[:, :, None, :, :], -jnp.inf))
        a = jnp.einsum('bhtd,bhsd,bhtsd->bhts', qc, kc, decay)
        o = jnp.einsum('bhts,bhse->bhte', a, vc) + jnp.einsum('bhtd,bhde->bhte', qc * jnp.exp(b), s)
        b_last = b[:, :, -1:, :]
        s_new = jnp.exp(b_last)[:, :, 0, :, None] * s + jnp.einsum('bhsd,bhse->bhde', kc * jnp.exp(b_last - b), vc)
        return s_new, o

    s_fin, o = lax.scan(step, s0, (chunks(q), chunks(log_f), chunks(k), chunks(v)))
    return o.transpose(1, 0, 3, 2, 4).reshape(bsz, n, h, dv), s_fin

def hgrn_direction(q, z, v, lb, s0, reverse):
    z = z.astype(jnp.float32)
    lb = lb.reshape(HG_HEADS, HG_DK)
    log_f = jnp.logaddexp(jnp.log(lb), jnp.log1p(-lb) + jax.nn.log_sigmoid(z))
    k = (1.0 - lb) * jax.nn.sigmoid(-z)
    if reverse:
        q, log_f, k, v = (jnp.flip(t, axis=1) for t in (q, log_f, k, v))
    o, s = hgrn_chunk_scan(q, log_f, k, v, s0)
    if reverse:
        o = jnp.flip(o, axis=1)
    return o, s

def hgrn_readout(o, g, norm_g):
    o = rmsnorm(o, norm_g.reshape(HG_HEADS, HG_DV))
    return o.reshape(o.shape[0], o.shape[1], HG_WIDTH).astype(g.dtype) * jax.nn.silu(g)

def depthwise_conv3(u, w):
    return lax.conv_general_dilated(u, w[:, None, :].astype(u.dtype), window_strides=(1,), padding='SAME',
                                    dimension_numbers=('NWC', 'WIO', 'NWC'), feature_group_count=CONV_WIDTH)

def gqa_softmax(qg, k, v):
    s = jnp.einsum('bqkgd,bskd->bkgqs', qg, k).astype(jnp.float32) * ATTN_SCALE
    p = jax.nn.softmax(s, axis=-1)
    return jnp.einsum('bkgqs,bskd->bqkgd', p.astype(v.dtype), v)

def attend_latent(q, k_lat, v_lat, k_ctx, v_ctx):
    bsz, n = q.shape[:2]
    k_all = jnp.concatenate([k_ctx, k_lat], axis=1)
    v_all = jnp.concatenate([v_ctx, v_lat], axis=1)
    qb = q.reshape(bsz, n // Q_BLOCK, Q_BLOCK, N_KV_HEADS, GQA_GROUP, HEAD_DIM).transpose(1, 0, 2, 3, 4, 5)
    o = lax.map(lambda qi: gqa_softmax(qi, k_all, v_all), qb)
    return o.transpose(1, 0, 2, 3, 4, 5).reshape(bsz, n, ATTN_WIDTH)

def attend_ctx(q, k, v):
    bsz, n = q.shape[:2]
    o = gqa_softmax(q.reshape(bsz, n, N_KV_HEADS, GQA_GROUP, HEAD_DIM), k, v)
    return o.reshape(bsz, n, ATTN_WIDTH)

def merge(pr, o_a, o_b, o_c, w_proj_a, w_proj_b, w_proj_c, w_out):
    ga, gb, gc = (jax.nn.sigmoid(t) for t in pr[11:14])
    y = ga * (o_a @ w_proj_a) + gb * (o_b @ w_proj_b) + gc * (o_c @ w_proj_c)
    return y @ w_out

def token_mixer(h_lat, h_ctx, w_in, lb_fwd, lb_bwd, hg_norm_g, conv_w, q_norm_g, k_norm_g,
                w_proj_a, w_proj_b, w_proj_c, w_out, cos, sin, ctx_out):
    pl = project(h_lat, w_in)
    pc = project(h_ctx, w_in)
    bsz = h_lat.shape[0]
    zero_state = jnp.zeros((bsz, HG_HEADS, HG_DK, HG_DV), jnp.float32)
    qc_h, ic_h = to_heads(pc[0], HG_DK), to_heads(pc[3], HG_DV)
    ql_h, il_h = to_heads(pl[0], HG_DK), to_heads(pl[3], HG_DV)
    oc_f, sc_f = hgrn_direction(qc_h, to_heads(pc[1], HG_DK), ic_h, lb_fwd, zero_state, False)
    oc_b, sc_b = hgrn_direction(qc_h, to_heads(pc[2], HG_DK), ic_h, lb_bwd, zero_state, True)
    ol_f, _ = hgrn_direction(ql_h, to_heads(pl[1], HG_DK), il_h, lb_fwd, sc_f, False)
    ol_b, _ = hgrn_direction(ql_h, to_heads(pl[2], HG_DK), il_h, lb_bwd, sc_b, True)
    a_lat = hgrn_readout(ol_f + ol_b, pl[4], hg_norm_g)
    b_lat = pl[5] * depthwise_conv3(pl[6] * pl[7], conv_w)
    q_l = apply_rope(rmsnorm(to_heads(pl[8], HEAD_DIM), q_norm_g), cos, sin)
    k_l = apply_rope(rmsnorm(to_heads(pl[9], HEAD_DIM), k_norm_g), cos, sin)
    v_l = to_heads(pl[10], HEAD_DIM)
    k_c = rmsnorm(to_heads(pc[9], HEAD_DIM), k_norm_g)
    v_c = to_heads(pc[10], HEAD_DIM)
    c_lat = attend_latent(q_l, k_l, v_l, k_c, v_c)
    y_lat = merge(pl, a_lat, b_lat, c_lat, w_proj_a, w_proj_b, w_proj_c, w_out)
    if not ctx_out:
        return y_lat, None
    a_ctx = hgrn_readout(oc_f + oc_b, pc[4], hg_norm_g)
    b_ctx = pc[5] * depthwise_conv3(pc[6] * pc[7], conv_w)
    q_c = rmsnorm(to_heads(pc[8], HEAD_DIM), q_norm_g)
    att_c = attend_ctx(q_c, k_c, v_c)
    y_ctx = merge(pc, a_ctx, b_ctx, att_c, w_proj_a, w_proj_b, w_proj_c, w_out)
    return y_lat, y_ctx

def expert_choice_ffn(h, router_w, w_gate, w_up, w_down):
    bsz, n, d = h.shape
    cap = CAPACITY_FACTOR * n // N_EXPERTS
    aff = jax.nn.softmax((h @ router_w).astype(jnp.float32), axis=-1)
    w_sel, idx = lax.top_k(aff.transpose(0, 2, 1), cap)
    xs = jax.vmap(lambda hb, ib: hb[ib])(h, idx)
    hid = jax.nn.silu(jnp.einsum('becd,edf->becf', xs, w_gate)) * jnp.einsum('becd,edf->becf', xs, w_up)
    ys = jnp.einsum('becf,efd->becd', hid, w_down) * w_sel[..., None].astype(h.dtype)
    return jax.vmap(lambda yb, ib: jnp.zeros((n, d), h.dtype).at[ib.reshape(-1)].add(yb.reshape(-1, d)))(ys, idx)

def first_inputs(seed: int = 0) -> dict:
    key = jax.random.key(seed)
    ks = jax.random.split(key, 23)

    def nrm(k, shape, scale):
        return jax.random.normal(k, shape, jnp.float32) * scale

    return {
        'x': nrm(ks[0], (BATCH, SEQ, D_MODEL), 1.0),
        'c': nrm(ks[1], (BATCH, D_MODEL), 1.0),
        'ctx': nrm(ks[2], (BATCH, CTX_LEN, D_MODEL), 1.0),
        'c_ctx': nrm(ks[3], (D_MODEL,), 1.0),
        'ada_w': nrm(ks[4], (DEPTH, D_MODEL, N_MOD * D_MODEL), 0.5 * D_MODEL ** -0.5),
        'ada_b': nrm(ks[5], (DEPTH, N_MOD * D_MODEL), 0.02),
        'norm1_g': 1.0 + nrm(ks[6], (DEPTH, D_MODEL), 0.1),
        'norm2_g': 1.0 + nrm(ks[7], (DEPTH, D_MODEL), 0.1),
        'w_in': nrm(ks[8], (DEPTH, D_MODEL, IN_WIDTH), D_MODEL ** -0.5),
        'hg_lb_logits': nrm(ks[9], (DEPTH, 2, HG_WIDTH), 1.0),
        'hg_norm_g': 1.0 + nrm(ks[10], (DEPTH, HG_WIDTH), 0.1),
        'conv_w': nrm(ks[11], (DEPTH, CONV_K, CONV_WIDTH), CONV_K ** -0.5),
        'q_norm_g': 1.0 + nrm(ks[12], (DEPTH, HEAD_DIM), 0.1),
        'k_norm_g': 1.0 + nrm(ks[13], (DEPTH, HEAD_DIM), 0.1),
        'w_proj_a': nrm(ks[14], (DEPTH, HG_WIDTH, D_MODEL), HG_WIDTH ** -0.5),
        'w_proj_b': nrm(ks[15], (DEPTH, CONV_WIDTH, D_MODEL), CONV_WIDTH ** -0.5),
        'w_proj_c': nrm(ks[16], (DEPTH, ATTN_WIDTH, D_MODEL), ATTN_WIDTH ** -0.5),
        'w_out': nrm(ks[17], (DEPTH, D_MODEL, D_MODEL), D_MODEL ** -0.5),
        'router_w': nrm(ks[18], (DEPTH, D_MODEL, N_EXPERTS), D_MODEL ** -0.5),
        'w_gate': nrm(ks[19], (DEPTH, N_EXPERTS, D_MODEL, EXPERT_FF), D_MODEL ** -0.5),
        'w_up': nrm(ks[20], (DEPTH, N_EXPERTS, D_MODEL, EXPERT_FF), D_MODEL ** -0.5),
        'w_down': nrm(ks[21], (DEPTH, N_EXPERTS, EXPERT_FF, D_MODEL), EXPERT_FF ** -0.5),
        'final_norm_g': 1.0 + nrm(ks[22], (D_MODEL,), 0.1),
    }

def first_block(x, c, ctx, c_ctx, ada_w, ada_b, norm1_g, norm2_g, w_in, hg_lb_logits, hg_norm_g, conv_w,
              q_norm_g, k_norm_g, w_proj_a, w_proj_b, w_proj_c, w_out, router_w, w_gate, w_up, w_down,
              final_norm_g):
    cos, sin = axial_rope_tables(x.shape[1])
    lb = jnp.cumsum(jax.nn.softmax(hg_lb_logits.astype(jnp.float32), axis=0), axis=0)
    lb = lb - lb[:1]
    h_ctx = ctx
    for l in range(DEPTH):
        ctx_out = l < DEPTH - 1
        sh_a, sc_a, g_a, sh_f, sc_f, g_f = modulation(c, ada_w[l], ada_b[l])
        csh_a, csc_a, cg_a, csh_f, csc_f, cg_f = modulation(c_ctx[None, :], ada_w[l], ada_b[l])
        y_lat, y_ctx = token_mixer(modulate(x, norm1_g[l], sh_a, sc_a), modulate(h_ctx, norm1_g[l], csh_a, csc_a),
                                   w_in[l], lb[l, 0], lb[l, 1], hg_norm_g[l], conv_w[l], q_norm_g[l], k_norm_g[l],
                                   w_proj_a[l], w_proj_b[l], w_proj_c[l], w_out[l], cos, sin, ctx_out)
        x = x + g_a * y_lat
        x = x + g_f * expert_choice_ffn(modulate(x, norm2_g[l], sh_f, sc_f), router_w[l], w_gate[l], w_up[l], w_down[l])
        if ctx_out:
            h_ctx = h_ctx + cg_a * y_ctx
            h_ctx = h_ctx + cg_f * expert_choice_ffn(modulate(h_ctx, norm2_g[l], csh_f, csc_f),
                                                     router_w[l], w_gate[l], w_up[l], w_down[l])
    return rmsnorm(x, final_norm_g)


CHUNK = 64
MIX_WIDTH = D_MODEL
POOL_WIDTH = MIX_WIDTH // 2
POOL_WINDOWS = (2, 4, 8, 16)
POOL_GROUPS = len(POOL_WINDOWS)
POOL_GROUP_DIM = POOL_WIDTH // POOL_GROUPS
DN_WIDTH = MIX_WIDTH - POOL_WIDTH
DN_HEADS = 4
DN_HEAD_DIM = DN_WIDTH // DN_HEADS
CONV_K_2 = 4
IN_COLS = POOL_WIDTH + 4 * DN_WIDTH + 2 * DN_HEADS
MEM_LEN = 256
XA_HEADS = 4
XA_HEAD_DIM = D_MODEL // XA_HEADS
D_FF = 4 * D_MODEL


def rmsnorm_2(x, g):
    xf = x.astype(jnp.float32)
    y = xf * lax.rsqrt(jnp.mean(xf * xf, axis=-1, keepdims=True) + EPS)
    return (y * g.astype(jnp.float32)).astype(x.dtype)

def l2norm(x):
    return x * lax.rsqrt(jnp.sum(x * x, axis=-1, keepdims=True) + EPS)

def pool_mixer(u, w_pool, pool_scale):
    B, S, _ = u.shape
    uf = u.astype(jnp.float32)
    csum = jnp.concatenate([jnp.zeros((B, 1, POOL_WIDTH), jnp.float32),
                            jnp.cumsum(uf, axis=1)], axis=1)
    t = jnp.arange(S)
    outs = []
    for gi, w in enumerate(POOL_WINDOWS):
        sl = slice(gi * POOL_GROUP_DIM, (gi + 1) * POOL_GROUP_DIM)
        c = csum[:, :, sl]
        lagged = jnp.concatenate([jnp.zeros((B, w - 1, POOL_GROUP_DIM), jnp.float32),
                                  c[:, :S - w + 1]], axis=1)
        cnt = jnp.minimum(t + 1, w).astype(jnp.float32)[None, :, None]
        outs.append((c[:, 1:] - lagged) / cnt - uf[:, :, sl])
    pooled = jnp.stack(outs, axis=2)
    mixed = jnp.einsum('bsgc,gcd->bsgd', pooled, w_pool.astype(jnp.float32))
    return (mixed.reshape(B, S, POOL_WIDTH) * pool_scale.astype(jnp.float32)).astype(u.dtype)

def causal_dwconv(x, w):
    K, C = w.shape
    return lax.conv_general_dilated(x, w[:, None, :], window_strides=(1,),
                                    padding=[(K - 1, 0)],
                                    dimension_numbers=('NWC', 'WIO', 'NWC'),
                                    feature_group_count=C)

def gated_delta_rule(q, k, v, g, beta):
    B, S, H, Dk = q.shape
    Dv = v.shape[-1]
    NC = S // CHUNK
    q = q * (Dk ** -0.5)

    def chunks(x):
        return x.reshape(B, NC, CHUNK, H, x.shape[-1]).transpose(0, 3, 1, 2, 4)

    qc, kc, vc = chunks(q), chunks(k), chunks(v)
    gc = jnp.cumsum(g.reshape(B, NC, CHUNK, H).transpose(0, 3, 1, 2), axis=-1)
    bc = beta.reshape(B, NC, CHUNK, H).transpose(0, 3, 1, 2)[..., None]

    tril = jnp.tril(jnp.ones((CHUNK, CHUNK), dtype=bool))
    strict = jnp.tril(jnp.ones((CHUNK, CHUNK), dtype=bool), k=-1)
    diff = gc[..., :, None] - gc[..., None, :]
    decay = jnp.where(tril, jnp.exp(jnp.where(tril, diff, 0.0)), 0.0)

    k_beta = kc * bc
    v_beta = vc * bc
    L = jnp.where(strict, jnp.einsum('bhnid,bhnjd->bhnij', k_beta, kc) * decay, 0.0)
    eye = jnp.eye(CHUNK, dtype=jnp.float32)
    T = lax.linalg.triangular_solve(eye + L, jnp.broadcast_to(eye, L.shape),
                                    left_side=True, lower=True)
    u = jnp.einsum('bhnij,bhnjd->bhnid', T, v_beta)
    w = jnp.einsum('bhnij,bhnjd->bhnid', T, k_beta * jnp.exp(gc)[..., None])
    attn = jnp.where(tril, jnp.einsum('bhnid,bhnjd->bhnij', qc, kc) * decay, 0.0)

    def step(state, inp):
        q_c, k_c, u_c, w_c, g_c, a_c = inp
        v_new = u_c - jnp.einsum('bhcd,bhde->bhce', w_c, state)
        o = (jnp.einsum('bhcd,bhde->bhce', q_c * jnp.exp(g_c)[..., None], state)
             + jnp.einsum('bhij,bhje->bhie', a_c, v_new))
        g_last = g_c[..., -1]
        k_dec = k_c * jnp.exp(g_last[..., None] - g_c)[..., None]
        state = state * jnp.exp(g_last)[..., None, None] + jnp.einsum('bhcd,bhce->bhde', k_dec, v_new)
        return state, o

    xs = (jnp.moveaxis(qc, 2, 0), jnp.moveaxis(kc, 2, 0), jnp.moveaxis(u, 2, 0),
          jnp.moveaxis(w, 2, 0), jnp.moveaxis(gc, 2, 0), jnp.moveaxis(attn, 2, 0))
    state0 = jnp.zeros((B, H, Dk, Dv), jnp.float32)
    _, o = lax.scan(step, state0, xs)
    return o.transpose(1, 0, 3, 2, 4).reshape(B, S, H, Dv)

def deltanet_mixer(q, k, v, z, b, a, conv_w, a_log, dt_bias, o_norm_g):
    B, S, _ = q.shape
    dtype = q.dtype
    qkv = jnp.concatenate([q, k, v], axis=-1).astype(jnp.float32)
    qkv = jax.nn.silu(causal_dwconv(qkv, conv_w.astype(jnp.float32)))
    qf, kf, vf = jnp.split(qkv, 3, axis=-1)
    qf = l2norm(qf.reshape(B, S, DN_HEADS, DN_HEAD_DIM))
    kf = l2norm(kf.reshape(B, S, DN_HEADS, DN_HEAD_DIM))
    vf = vf.reshape(B, S, DN_HEADS, DN_HEAD_DIM)
    beta = jax.nn.sigmoid(b.astype(jnp.float32))
    g = -jnp.exp(a_log.astype(jnp.float32)) * jax.nn.softplus(a.astype(jnp.float32) + dt_bias.astype(jnp.float32))
    o = gated_delta_rule(qf, kf, vf, g, beta)
    o = o * lax.rsqrt(jnp.mean(o * o, axis=-1, keepdims=True) + EPS) * o_norm_g.astype(jnp.float32)
    o = o * jax.nn.silu(z.astype(jnp.float32).reshape(B, S, DN_HEADS, DN_HEAD_DIM))
    return o.reshape(B, S, DN_WIDTH).astype(dtype)

def memory_cross_attention(h, m, w_q, w_k, w_v, w_o):
    B, S, _ = h.shape
    M = m.shape[1]
    q = (h @ w_q).reshape(B, S, XA_HEADS, XA_HEAD_DIM)
    k = (m @ w_k).reshape(B, M, XA_HEADS, XA_HEAD_DIM)
    v = (m @ w_v).reshape(B, M, XA_HEADS, XA_HEAD_DIM)
    s = jnp.einsum('bshd,bmhd->bhsm', q, k).astype(jnp.float32) * (XA_HEAD_DIM ** -0.5)
    p = jax.nn.softmax(s, axis=-1).astype(v.dtype)
    o = jnp.einsum('bhsm,bmhd->bshd', p, v).reshape(B, S, D_MODEL)
    return o @ w_o

def sqrelu_mlp(h, w_up, w_down):
    a = jax.nn.relu(h @ w_up)
    return (a * a) @ w_down

def second_inputs(seed: int = 0) -> dict:
    key = jax.random.key(seed)
    ks = jax.random.split(key, 24)

    def nrm(k, shape, scale):
        return jax.random.normal(k, shape, jnp.float32) * scale

    def gain(k, shape):
        return 1.0 + 0.05 * jax.random.normal(k, shape, jnp.float32)

    L = DEPTH
    return {
        "x": nrm(ks[0], (BATCH, SEQ, D_MODEL), 1.0),
        "mem": nrm(ks[1], (BATCH, MEM_LEN, D_MODEL), 1.0),
        "norm_mix_g": gain(ks[2], (L, D_MODEL)),
        "w_in": nrm(ks[3], (L, D_MODEL, IN_COLS), D_MODEL ** -0.5),
        "w_pool": nrm(ks[4], (L, POOL_GROUPS, POOL_GROUP_DIM, POOL_GROUP_DIM), POOL_GROUP_DIM ** -0.5),
        "pool_scale": gain(ks[5], (L, POOL_WIDTH)),
        "conv_w": nrm(ks[6], (L, CONV_K_2, 3 * DN_WIDTH), CONV_K_2 ** -0.5),
        "a_log": jnp.log(jax.random.uniform(ks[7], (L, DN_HEADS), jnp.float32, 1.0, 16.0)),
        "dt_bias": 0.5 + 0.1 * jax.random.normal(ks[8], (L, DN_HEADS), jnp.float32),
        "dn_out_norm_g": gain(ks[9], (L, DN_HEAD_DIM)),
        "w_out": nrm(ks[10], (L, MIX_WIDTH, D_MODEL), MIX_WIDTH ** -0.5),
        "norm_xattn_g": gain(ks[11], (L, D_MODEL)),
        "mem_norm_g": gain(ks[12], (L, D_MODEL)),
        "w_xq": nrm(ks[13], (L, D_MODEL, D_MODEL), D_MODEL ** -0.5),
        "w_xk": nrm(ks[14], (L, D_MODEL, D_MODEL), D_MODEL ** -0.5),
        "w_xv": nrm(ks[15], (L, D_MODEL, D_MODEL), D_MODEL ** -0.5),
        "w_xo": nrm(ks[16], (L, D_MODEL, D_MODEL), D_MODEL ** -0.5),
        "norm_mlp_g": gain(ks[17], (L, D_MODEL)),
        "w_up": nrm(ks[18], (L, D_MODEL, D_FF), D_MODEL ** -0.5),
        "w_down": nrm(ks[19], (L, D_FF, D_MODEL), D_FF ** -0.5),
        "final_norm_g": gain(ks[20], (D_MODEL,)),
    }

def second_block(x, mem, norm_mix_g, w_in, w_pool, pool_scale, conv_w, a_log, dt_bias,
              dn_out_norm_g, w_out, norm_xattn_g, mem_norm_g, w_xq, w_xk, w_xv, w_xo,
              norm_mlp_g, w_up, w_down, final_norm_g):
    P, W, H = POOL_WIDTH, DN_WIDTH, DN_HEADS
    h = x
    for l in range(DEPTH):
        hn = rmsnorm_2(h, norm_mix_g[l])
        proj = hn @ w_in[l]
        u_pool = proj[..., :P]
        q = proj[..., P:P + W]
        k = proj[..., P + W:P + 2 * W]
        v = proj[..., P + 2 * W:P + 3 * W]
        z = proj[..., P + 3 * W:P + 4 * W]
        b = proj[..., P + 4 * W:P + 4 * W + H]
        a = proj[..., P + 4 * W + H:]
        y_pool = pool_mixer(u_pool, w_pool[l], pool_scale[l])
        y_dn = deltanet_mixer(q, k, v, z, b, a, conv_w[l], a_log[l], dt_bias[l], dn_out_norm_g[l])
        h = h + jnp.concatenate([y_pool, y_dn], axis=-1) @ w_out[l]
        m = rmsnorm_2(mem, mem_norm_g[l])
        h = h + memory_cross_attention(rmsnorm_2(h, norm_xattn_g[l]), m, w_xq[l], w_xk[l], w_xv[l], w_xo[l])
        h = h + sqrelu_mlp(rmsnorm_2(h, norm_mlp_g[l]), w_up[l], w_down[l])
    return rmsnorm_2(h, final_norm_g)


def setup_inputs(seed=0):
    out = dict(first_inputs(seed))
    for name, value in second_inputs(seed + 1).items():
        if name != "x":
            out[name + "_2"] = value
    return out


def reference(
    x, c, ctx, c_ctx, ada_w, ada_b, norm1_g, norm2_g, w_in, hg_lb_logits, hg_norm_g, conv_w,
    q_norm_g, k_norm_g, w_proj_a, w_proj_b, w_proj_c, w_out, router_w, w_gate, w_up, w_down,
    final_norm_g, mem_2, norm_mix_g_2, w_in_2, w_pool_2, pool_scale_2, conv_w_2, a_log_2,
    dt_bias_2, dn_out_norm_g_2, w_out_2, norm_xattn_g_2, mem_norm_g_2, w_xq_2, w_xk_2, w_xv_2,
    w_xo_2, norm_mlp_g_2, w_up_2, w_down_2, final_norm_g_2,
):
    x = first_block(
        x, c, ctx, c_ctx, ada_w, ada_b, norm1_g, norm2_g, w_in, hg_lb_logits, hg_norm_g, conv_w,
        q_norm_g, k_norm_g, w_proj_a, w_proj_b, w_proj_c, w_out, router_w, w_gate, w_up, w_down,
        final_norm_g,
    )
    return second_block(
        x, mem_2, norm_mix_g_2, w_in_2, w_pool_2, pool_scale_2, conv_w_2, a_log_2, dt_bias_2,
        dn_out_norm_g_2, w_out_2, norm_xattn_g_2, mem_norm_g_2, w_xq_2, w_xk_2, w_xv_2, w_xo_2,
        norm_mlp_g_2, w_up_2, w_down_2, final_norm_g_2,
    )


_drawn_inputs = setup_inputs


def setup_inputs(seed=0):
    import zlib

    import numpy as np

    out = dict(_drawn_inputs(seed))
    spreads = {}
    factors = {'ctx': 6.029,
     'c_ctx': 2.868,
     'hg_norm_g': 4.095,
     'q_norm_g': 8.0,
     'k_norm_g': 8.0,
     'dt_bias_2': 64.0,
     'dn_out_norm_g_2': 4.206,
     'norm_xattn_g_2': 8.0,
     'mem_norm_g_2': 8.0,
     'a_log_2': 8.0,
     'norm_mlp_g_2': 6.505}
    for name, (base, spread) in spreads.items():
        noise = np.random.default_rng([zlib.crc32(name.encode()), seed]).standard_normal(out[name].shape)
        drawn = base * np.exp(spread * noise) if base else spread * noise
        out[name] = jnp.asarray(drawn.astype(out[name].dtype))
    for name, factor in factors.items():
        out[name] = (out[name] * factor).astype(out[name].dtype)
    return out
```

```python
from contextlib import ExitStack
import numpy as np
import concourse.bass as bass
from concourse import mybir

F32 = mybir.dt.float32
I32 = mybir.dt.int32
ALU = mybir.AluOpType
ACT = mybir.ActivationFunctionType
AX = mybir.AxisListType.X

P = 128
D = 1024
KC = D // P
S = 512
C = 256
T = C + S
LT, CT_ = S // P, C // P
NT = T // P
EPS = 1e-6
BANK = 512
LEVELS = 7
HEADS = 8
NE, CAP = 16, 64
DNH = 4

COL = dict(q=0, zf=1024, zb=2048, i=3072, g=4096, b5=5120, b6=6144, b7=7168, aq=8192, ak=9216, av=9472,
           ga=9728, gb=10752, gc=11776)


def layout():
    cols, parts, at = {}, [], 0

    def put(name, a):
        nonlocal at
        a = np.asarray(a, np.float32).reshape(P, -1)
        cols[name] = (at, a.shape[1])
        parts.append(a)
        at += a.shape[1]

    r = np.arange(P)
    put("ident", np.eye(P))
    put("ones", np.ones((P, P)))
    put("ones_half", np.kron(np.eye(2), np.ones((64, 64))))
    rot = np.zeros((P, P))
    rot[r[1::2], r[0::2]] = -1.0
    rot[r[0::2], r[1::2]] = 1.0
    put("rot", rot)
    pos = np.arange(S)
    row = (pos // 64).astype(np.float32)
    col = (pos % 64).astype(np.float32)
    inv = (np.float32(10000.0) ** (-np.arange(0, 32, 2, dtype=np.float32) / np.float32(32))).astype(np.float32)
    ang = np.concatenate([row[:, None] * inv, col[:, None] * inv], -1).astype(np.float32)
    ang = ang[:, (r % 64) // 2].T
    put("cos", np.cos(ang))
    put("sin", np.sin(ang))
    masks = [np.eye(P)]
    for l in range(LEVELS):
        h = 1 << l
        same = (r[:, None] // (2 * h)) == (r[None, :] // (2 * h))
        masks.append(same & ((r[:, None] // h) != (r[None, :] // h)))
    put("masks", np.stack(masks, 1))
    put("upper", r[:, None] <= r[None, :])
    put("lower_strict", r[:, None] > r[None, :])
    put("off_diagonal", 1 - np.eye(P))
    put("slots", np.tile(np.arange(CAP), (P, 1)))
    put("eps", np.full((P, 1), EPS))
    put("restart", np.tile((pos % P != 0), (P, 1)))
    sel = np.zeros((P, 8, P))
    for k in range(8):
        sel[k, k, :] = 1.0
    put("row_of", sel)
    counts = np.stack([1.0 / np.minimum(pos + 1, w) for w in (2, 4, 8, 16)])
    small = at
    put("counts", np.tile(counts.reshape(1, -1), (P, 1)))
    return cols, np.concatenate(parts, 1), small


CONST_COLS, CONST, CONST_SMALL = layout()


def view(ap, offset, dims):
    return bass.AP(ap.tensor, ap.offset + offset, [tuple(ap.ap[0])] + [tuple(d) for d in dims])


def bcast(ap, n):
    return ap.unsqueeze(len(ap.shape)).to_broadcast(list(ap.shape) + [n])


def bmid(ap, n):
    return view(ap, 0, [(0, n), tuple(ap.ap[-1])])


def wait(eng, sem, n):
    if not (isinstance(n, int) and n <= 0):
        eng.wait_ge(sem, n)


class Carve:

    def __init__(self, arena, lo, hi):
        self.arena, self.at, self.hi = arena, lo, hi

    def take(self, *dims):
        n = int(np.prod(dims))
        assert self.at + n <= self.hi, (self.at, n, self.hi)
        ap = self.arena[:, self.at:self.at + n]
        self.at += n
        if len(dims) == 2:
            ap = ap.rearrange("p (a b) -> p a b", a=dims[0])
        if len(dims) == 3:
            ap = ap.rearrange("p (a b c) -> p a b c", a=dims[0], b=dims[1])
        return ap


class WeightStream:

    def __init__(self, sem_full, sem_used):
        self.full, self.used = sem_full, sem_used
        self.phases, self.total = {}, 0
        self.last = []
        self.count = [0] * len(sem_full)
        self.slot_last = [-1] * len(sem_full)

    def phase(self, name, iters, units, slots=None):
        n, first, again = len(units), [], []
        slots = slots or list(range(n))
        for u, (_, _, lo, hi) in enumerate(units):
            over = [x for a, b, x in self.last if a < hi and lo < b] + [self.slot_last[slots[u]]]
            first.append(max(over) + 1)
            same = [v for v in range(n) if slots[v] == slots[u] or (units[v][2] < hi and lo < units[v][3])]
            before = [v for v in same if v < u]
            again.append(self.total + 1 + (max(before) if before else max(same) - n))
            self.last = [(a, b, x) for a, b, x in self.last if not (lo <= a and b <= hi)]
            self.last.append((lo, hi, self.total + u))
            self.slot_last[slots[u]] = self.total + u
        self.phases[name] = dict(iters=iters, units=units, base=self.total, first=first, again=again, slots=slots,
                                 full=list(self.count))
        for u in range(n):
            self.count[slots[u]] += 16 * iters
        shift = (iters - 1) * n
        self.slot_last = [x + shift if x >= self.total else x for x in self.slot_last]
        self.last = [(a, b, x + shift if x >= self.total else x) for a, b, x in self.last]
        self.total += n * iters

    def load(self, eng, name):
        ph = self.phases[name]
        n = len(ph["units"])
        for u, (src, dst, _, _) in enumerate(ph["units"]):
            wait(eng, self.used, ph["first"][u])
            eng.dma_start(dst, src(0)).then_inc(self.full[ph["slots"][u]], 16)
        if ph["iters"] > 1:
            with eng.Fori(1, ph["iters"]) as i:
                for u, (src, dst, _, _) in enumerate(ph["units"]):
                    eng.wait_ge(self.used, i * n + ph["again"][u])
                    eng.dma_start(dst, src(i)).then_inc(self.full[ph["slots"][u]], 16)

    def arrived(self, pe, name, i, u):
        ph = self.phases[name]
        s = ph["slots"][u]
        per = ph["slots"].count(s)
        pe.wait_ge(self.full[s], i * (16 * per) + (ph["full"][s] + 16 * (ph["slots"][:u].count(s) + 1)))

    def dst(self, name, u):
        return self.phases[name]["units"][u][1]


def mixed_block_kernel(nc, A, out):
    ctx = ExitStack()
    with ctx:
        sems = {}

        def sem(name):
            if name not in sems:
                sems[name] = ctx.enter_context(nc.semaphore(name))
            return sems[name]

        COLS = 53000
        arena = ctx.enter_context(nc.sbuf_tensor("arena", [P, COLS], F32))
        psum = ctx.enter_context(nc.psum_tensor("psum", [P, 8, BANK], F32))

        fix = Carve(arena, 0, 5230)
        consts = fix.take(CONST_SMALL)

        def const(name):
            at, n = CONST_COLS[name]
            return consts[:, at:at + n]

        ident, ones, ones_half, rot = (const(n) for n in ("ident", "ones", "ones_half", "rot"))
        cos, sin, eps, slots = (const(n) for n in ("cos", "sin", "eps", "slots"))
        masks = const("masks").rearrange("p (l t) -> p l t", l=LEVELS + 1)
        vec1 = fix.take(P)
        vec2 = fix.take(P)
        silu_c = fix.take(KC, 2)
        mod = fix.take(48, 2)
        scale1 = fix.take(KC, 2)
        scale2 = fix.take(KC)
        N1, N2G, HGN, FIN1, CONV1, ADAB, CVEC, QN, KN, DNN = 0, 8, 16, 24, 32, 56, 104, 120, 121, 122
        MIXN, XN, MEMN, MLPN, FIN2, PSC, CONV2 = 0, 8, 16, 24, 32, 40, 44
        SH_A, SC_A, G_A, SH_F, SC_F, G_F = range(6)

        lo = 5230
        XT = Carve(arena, lo, lo + 4096).take(KC, S)
        lo += 4096
        HT_LO = lo
        HT = Carve(arena, lo, lo + 6144).take(KC, T)
        lo += 6144
        BT_LO = lo
        bT = Carve(arena, lo, lo + 4096).take(KC, S)
        lo += 4096
        aT = Carve(arena, lo, lo + 4096).take(KC, S)
        lo += 4096
        CT_LO = lo
        cT = Carve(arena, lo, lo + 4096).take(KC, S)
        yT = Carve(arena, lo + 4096, lo + 8192).take(KC, S)
        lo += 8192
        RING_LO = COLS - 16384
        UNIT_LO = COLS - 8192
        EXTRA = (lo, RING_LO)
        ring = Carve(arena, RING_LO, COLS).take(16384)

        def unit_place(u):
            at = 8192 + 1024 * u
            return ring[:, at:at + 1024].rearrange("p (k n) -> p k n", k=KC), at, at + 1024

        def quad_place(u):
            return ring[:, 4096 * u:4096 * u + 4096].rearrange("p (k n) -> p k n", k=KC), 4096 * u, 4096 * u + 4096

        def cut(w, n):
            return w.rearrange("(k p) (c n) -> c p k n", p=P, n=n)

        ws = WeightStream([sem(f"weights_full_{u}") for u in range(8)], sem("weights_used"))

        ada = cut(A["ada_w"][0], 512)
        ws.phase("mod", 3, [((lambda i, u=u: ada[i * 4 + u]),) + quad_place(u) for u in range(4)])

        w_in1 = cut(A["w_in"][0], P)
        HG_UNITS = ["b6", "b7", "b5", "g", "zf", "zb", "i", "q"]
        ws.phase("hg", 8, [((lambda i, c=c: w_in1[i + COL[c] // P]),) + unit_place(u)
                           for u, c in enumerate(HG_UNITS)])

        ctx_raw = Carve(arena, EXTRA[0] + S, EXTRA[1]).take(KC, C)

        stage = Carve(arena, BT_LO, COLS)
        x_tok = stage.take(LT, D)
        c_tok = stage.take(CT_, D)
        rows1 = stage.take(P)
        rows2 = stage.take(P)
        assert stage.at <= RING_LO

        def sp_setup(sp):
            sp.dma_start(consts, A["const_table"][:, 0:CONST_SMALL]).then_inc(sem("consts_in"), 16)
            r = 0
            plan = [("norm1_g", 8), ("norm2_g", 8), ("hg_norm_g", 8), ("final_norm_g", 8), ("conv_w", 24),
                    ("ada_b", 48), ("c", 8), ("c_ctx", 8), ("q_norm_g", 0), ("k_norm_g", 0), ("dn_out_norm_g_2", 1)]
            n = 0
            for name, k in plan:
                if k == 0:
                    for half in range(2):
                        sp.dma_start(rows1[r:r + 1, 64 * half:64 * half + 64], A[name]).then_inc(sem("rows_in"), 16)
                        n += 1
                    r += 1
                    continue
                flat = A[name]
                if name == "c_ctx" or name == "final_norm_g":
                    src = flat.rearrange("(r n) -> r n", n=P)
                elif name == "conv_w":
                    src = flat[0].rearrange("t (r n) -> (t r) n", n=P)
                else:
                    src = flat.rearrange("l (r n) -> (l r) n", n=P)
                sp.dma_start(rows1[r:r + k, :], src).then_inc(sem("rows_in"), 16)
                n += 1
                r += k
            r = 0
            for name, k in [("norm_mix_g_2", 8), ("norm_xattn_g_2", 8), ("mem_norm_g_2", 8), ("norm_mlp_g_2", 8),
                            ("final_norm_g_2", 8), ("pool_scale_2", 4), ("conv_w_2", 48)]:
                flat = A[name]
                if name == "final_norm_g_2":
                    src = flat.rearrange("(r n) -> r n", n=P)
                elif name == "conv_w_2":
                    src = flat[0].rearrange("t (r n) -> (t r) n", n=P)
                else:
                    src = flat.rearrange("l (r n) -> (l r) n", n=P)
                sp.dma_start(rows2[r:r + k, :], src).then_inc(sem("rows_in"), 16)
                n += 1
                r += k
            assert n == N_ROW_LOADS, n
            sp.dma_start(x_tok, A["x"][0].rearrange("(t p) d -> p t d", p=P)).then_inc(sem("x_in"), 16)
            sp.dma_start(c_tok, A["ctx"][0].rearrange("(t p) d -> p t d", p=P)).then_inc(sem("ctx_in"), 16)

        N_ROW_LOADS = 20

        def pe_setup(pe):
            pe.wait_ge(sem("consts_in"), 16)
            pe.wait_ge(sem("rows_in"), 16 * N_ROW_LOADS)
            pe.transpose(psum[:, 0, 0:123], rows1[0:123, :], ident[0:123, 0:123])
            pe.transpose(psum[:, 0, 128:128 + 92], rows2[0:92, :], ident[0:92, 0:92]).then_inc(sem("rows_turned"), 1)
            n = 0
            for k in range(KC):
                for src, tiles in ((x_tok, LT), (c_tok, CT_)):
                    if n == 0:
                        pe.wait_ge(sem("x_in"), 16)
                    if n == 1:
                        pe.wait_ge(sem("ctx_in"), 16)
                    wait(pe, sem("turn_out"), n - 2)
                    for t in range(tiles):
                        mm = pe.transpose(psum[:, 1 + n % 3, t * P:(t + 1) * P], src[:, t, k * P:(k + 1) * P], ident)
                    mm.then_inc(sem("turned"), 1)
                    n += 1

        def dve_setup(dve):
            dve.wait_ge(sem("rows_turned"), 1)
            dve.tensor_copy(vec1[:, 0:123], psum[:, 0, 0:123])
            dve.tensor_copy(vec2[:, 0:92], psum[:, 0, 128:128 + 92]).then_inc(sem("vectors"), 1)
            n = 0
            for k in range(KC):
                for dst, tiles in ((XT[:, k, :], LT), (ctx_raw[:, k, :], CT_)):
                    dve.wait_ge(sem("turned"), n + 1)
                    dve.tensor_copy(dst, psum[:, 1 + n % 3, 0:tiles * P]).then_inc(sem("turn_out"), 1)
                    n += 1

        def act_setup(act):
            act.wait_ge(sem("vectors"), 1)
            act.activation(silu_c.rearrange("p k w -> p w k"),
                           vec1[:, CVEC:CVEC + 16].rearrange("p (w k) -> p w k", w=2), ACT.Silu).then_inc(sem("silu_c"), 1)

        mod_rows = Carve(arena, CT_LO, CT_LO + 6144).take(12, 512)

        def pe_mod(pe):
            pe.wait_ge(sem("silu_c"), 1)
            with pe.Fori(0, 3) as i:
                for u in range(4):
                    ws.arrived(pe, "mod", i, u)
                    pe.wait_ge(sem("mod_rows_out"), i * 4 + (u + 1))
                    w = ws.dst("mod", u)
                    for k in range(KC):
                        mm = pe.matmul(psum[0:2, 4 + u, :], silu_c[:, k, :], w[:, k, :], start=(k == 0), stop=(k == KC - 1))
                    mm.then_inc(sem("weights_used"), 1)
            pe.wait_ge(sem("mod_rows_out"), 16)
            for m in range(48):
                mm = pe.transpose(psum[:, 0, 2 * m:2 * m + 2], mod_rows[0:2, m // 4, (m % 4) * P:(m % 4 + 1) * P],
                                  ident[0:2, 0:2])
            mm.then_inc(sem("mod_turned"), 1)

        def act_mod(act):
            act.sem_inc(sem("mod_rows_out"), 4)
            with act.Fori(0, 3) as i:
                for u in range(4):
                    act.wait_ge(sem("weights_used"), i * 4 + (u + 1))
                    act.activation(mod_rows[0:2, i * 4 + u, :], psum[0:2, 4 + u, :], ACT.Copy).then_inc(sem("mod_rows_out"), 1)

        def dve_mod(dve):
            dve.wait_ge(sem("mod_turned"), 1)
            dve.tensor_tensor(mod, psum[:, 0, 0:96].rearrange("p (m w) -> p m w", w=2),
                              bcast(vec1[:, ADAB:ADAB + 48], 2), ALU.add)
            dve.drain()
            for w in range(2):
                dve.scalar_tensor_tensor(scale1[:, :, w], mod[:, SC_A * KC:SC_A * KC + KC, w], 1.0, vec1[:, N1:N1 + KC],
                                         ALU.add, ALU.mult)
            dve.scalar_tensor_tensor(scale2, mod[:, SC_F * KC:SC_F * KC + KC, 0], 1.0, vec1[:, N2G:N2G + KC],
                                     ALU.add, ALU.mult)
            dve.drain()
            dve.sem_inc(sem("mod_ready"), 1)

        NORMS = []

        def norm(src, dst, n, scale, shift, bank, work, before=()):
            NORMS.append(dict(src=src, dst=dst, n=n, scale=scale, shift=shift, bank=bank, work=work, before=before))
            return len(NORMS) - 1

        def act_norm(act, m):
            z = NORMS[m]
            for s, n in z["before"]:
                act.wait_ge(sem(s), n)
            act.activation(z["dst"], z["src"], ACT.Square).then_inc(sem("squares"), 1)
            act.wait_ge(sem("sums"), m + 1)
            wait(act, sem("normed"), m)
            act.activation(z["work"][:, 0:z["n"]], psum[:, z["bank"], 0:z["n"]], ACT.Sqrt, bias=eps, scale=1.0 / D)\
               .then_inc(sem("roots"), 1)

        def pe_norm(pe, m):
            z = NORMS[m]
            pe.wait_ge(sem("squares"), m + 1)
            for k in range(KC):
                mm = pe.matmul(psum[:, z["bank"], 0:z["n"]], ones, z["dst"][:, k, :], start=(k == 0), stop=(k == KC - 1))
            mm.then_inc(sem("sums"), 1)

        def dve_norm(dve, m):
            z = NORMS[m]
            n = z["n"]
            r = z["work"][:, 0:n]
            dve.wait_ge(sem("roots"), m + 1)
            dve.reciprocal(r, r)
            dve.drain()
            dve.tensor_tensor(z["dst"], z["src"], bmid(r, KC), ALU.mult)
            dve.drain()
            for k in range(KC):
                if z["shift"] is None:
                    dve.tensor_scalar(z["dst"][:, k, :], z["dst"][:, k, :], z["scale"](k), None, ALU.mult)
                else:
                    dve.tensor_scalar(z["dst"][:, k, :], z["dst"][:, k, :], z["scale"](k), z["shift"](k),
                                      ALU.mult, ALU.add)
            dve.drain()
            dve.sem_inc(sem("normed"), 1)

        norm_work = Carve(arena, EXTRA[0], EXTRA[1]).take(S)
        n_ctx = norm(ctx_raw, HT[:, :, 0:C], C, lambda k: scale1[:, k, 1:2], lambda k: mod[:, SH_A * KC + k, 1:2],
                     5, norm_work)
        n_lat = norm(XT, HT[:, :, C:T], S, lambda k: scale1[:, k, 0:1], lambda k: mod[:, SH_A * KC + k, 0:1],
                     6, norm_work)
        NORMS[n_ctx]["before"] = (("turn_out", 2 * KC),)

        hgp = Carve(arena, CT_LO, UNIT_LO)
        hp_q = hgp.take(S)
        hp_f = hgp.take(2, T)
        hp_k = hgp.take(2, T)
        hp_v = hgp.take(NT, P)
        hp_g = hgp.take(S)
        cv_b6 = hgp.take(S)
        cv_u = hgp.take(S)
        cv_y = hgp.take(S)
        hw_q0 = hgp.take(S)
        hw_q = hgp.take(2, S)
        hw_k = hgp.take(2, T)
        hw_v = hgp.take(NT, P)
        hw_g = hgp.take(S)
        hw_f = [hgp.take(2, T >> l) for l in range(LEVELS + 1)]
        hw_a = hgp.take(LT, P)
        hw_kt = hgp.take(10, P)
        hw_s = hgp.take(10, P)
        hw_sq = hgp.take(S)
        hw_r = hgp.take(S)
        hw_o = hgp.take(S)
        FWD_TILES = [0, 1, 2, 3, 4]
        BWD_TILES = [1, 0, 5, 4, 3]
        PIECES = [(0, "b6"), (1, "b7"), (2, "b5"), (3, "g"), (4, "fc"), (4, "fl"), (5, "bc"), (5, "bl"),
                  (6, "v0"), (6, "v1"), (7, "q")]

        def bank_uses(i, j):
            per = 6 if j % 2 == 0 else 5
            return i * per + j // 2

        def pe_piece(pe, i, j):
            u, what = PIECES[j]
            if j == 0 or PIECES[j - 1][0] != u:
                ws.arrived(pe, "hg", i, u)
            wait(pe, sem(f"piece_out_{j % 2}"), bank_uses(i, j))
            w = ws.dst("hg", u)
            bank = psum[:, j % 2, :]

            def first(mm):
                if j > 0 and PIECES[j - 1][0] != u:
                    mm.then_inc(sem("weights_used"), 1)

            if what[0] == "v":
                for t in range(3):
                    tile = 3 * int(what[1]) + t
                    for k in range(KC):
                        mm = pe.matmul(bank[:, t * P:(t + 1) * P], HT[:, k, tile * P:(tile + 1) * P], w[:, k, :],
                                       start=(k == 0), stop=(k == KC - 1))
                        if t == 0 and k == 0:
                            first(mm)
            else:
                a, b = (0, C) if what in ("fc", "bc") else (C, T)
                for k in range(KC):
                    mm = pe.matmul(bank[:, 0:b - a], w[:, k, :], HT[:, k, a:b], start=(k == 0), stop=(k == KC - 1))
                    if k == 0:
                        first(mm)
            mm.then_inc(sem(f"piece_{j % 2}"), 1)
            if j == len(PIECES) - 1:
                pe.wait_ge(sem(f"piece_{j % 2}"), bank_uses(i, j) + 1)
                pe.sem_inc(sem("weights_used"), 1)

        def act_piece(act, i, j):
            u, what = PIECES[j]
            bank = psum[:, j % 2, :]
            act.wait_ge(sem(f"piece_{j % 2}"), bank_uses(i, j) + 1)
            if j == 3:
                wait(act, sem("head_taken"), i)
            if j == 0:
                wait(act, sem("conv_read"), i)
            out_ = sem(f"piece_out_{j % 2}")
            if what == "b6":
                act.activation(cv_b6, bank, ACT.Copy).then_inc(out_, 1)
            elif what == "g":
                act.activation(hp_g, bank, ACT.Silu).then_inc(out_, 1)
            elif what in ("fc", "fl", "bc", "bl"):
                d = "fb".index(what[0])
                a, b = (0, C) if what[1] == "c" else (C, T)
                act.activation(hp_f[:, d, a:b], bank[:, 0:b - a], ACT.Sigmoid)
                act.activation(hp_k[:, d, a:b], bank[:, 0:b - a], ACT.Sigmoid, scale=-1.0).then_inc(out_, 1)
            elif what[0] == "v":
                h = int(what[1])
                act.activation(hp_v[:, 3 * h:3 * h + 3, :], bank[:, 0:3 * P].rearrange("p (t e) -> p t e", t=3),
                               ACT.Copy).then_inc(out_, 1)
            else:
                act.activation(hp_q, bank, ACT.Copy).then_inc(out_, 1)

        ACT_PIECES = [0, 3, 4, 5, 6, 7, 8, 9, 10]

        def dve_conv1(dve, i):
            dve.wait_ge(sem("piece_1"), bank_uses(i, 1) + 1)
            dve.wait_ge(sem("piece_out_0"), bank_uses(i, 0) + 1)
            dve.tensor_tensor(cv_u, cv_b6, psum[:, 1, :], ALU.mult)
            dve.drain()
            dve.sem_inc(sem("piece_out_1"), 1)
            dve.sem_inc(sem("conv_read"), 1)
            tap = [vec1[:, CONV1 + 8 * t:CONV1 + 8 * t + 8] for t in range(3)]
            dve.tensor_scalar(cv_y, cv_u, tap[1][:, bass.ds(i, 1)], None, ALU.mult)
            dve.drain()
            dve.scalar_tensor_tensor(cv_y[:, 1:S], cv_u[:, 0:S - 1], tap[0][:, bass.ds(i, 1)], cv_y[:, 1:S], ALU.mult, ALU.add)
            dve.drain()
            dve.scalar_tensor_tensor(cv_y[:, 0:S - 1], cv_u[:, 1:S], tap[2][:, bass.ds(i, 1)], cv_y[:, 0:S - 1],
                                     ALU.mult, ALU.add)
            dve.drain()

        def dve_conv2(dve, i):
            dve.wait_ge(sem("piece_0"), bank_uses(i, 2) + 1)
            dve.tensor_tensor(bT[:, i, :], cv_y, psum[:, 0, :], ALU.mult).then_inc(sem("piece_out_0"), 1)

        def pe_level(pe, i, l):
            n = i * 8 + (l - 8)
            if l == 0:
                pe.wait_ge(sem("head_taken"), i)
            else:
                pe.wait_ge(sem("levels_out"), n)
            bank = psum[:, 2 + l % 2, :]
            for t in range(LT):
                o = bank[:, t * P:(t + 1) * P]
                if l == 0:
                    q = hw_q0[:, t * P:(t + 1) * P]
                    pe.matmul(o, hw_k[:, 0, C + t * P:C + (t + 1) * P], q, start=True, stop=False)
                    mm = pe.matmul(o, hw_k[:, 1, C + t * P:C + (t + 1) * P], q, start=False, stop=True)
                else:
                    h = 1 << (l - 1)
                    half = [(2 * h, P // (2 * h)), (1, h)]
                    pe.matmul(view(o, h, half), hw_k[:, 0, C + t * P:C + (t + 1) * P],
                              view(hw_q, S + t * P + h, half), start=True, stop=True)
                    mm = pe.matmul(view(o, 0, half), hw_k[:, 1, C + t * P:C + (t + 1) * P],
                                   view(hw_q, t * P, half), start=True, stop=True)
            mm.then_inc(sem("levels"), 1)

        def dve_take(dve, i):
            dve.wait_ge(sem("piece_out_0"), i * 6)
            dve.wait_ge(sem("piece_out_1"), i * 5)
            dve.tensor_tensor(hw_q[:, 1, :], hp_q, hp_f[:, 0, C:T], ALU.mult)
            dve.tensor_tensor(hw_q[:, 0, :], hp_q, hp_f[:, 1, C:T], ALU.mult)
            dve.tensor_copy(hw_q0, hp_q)
            dve.tensor_copy(hw_k, hp_k)
            dve.tensor_copy(hw_f[0], hp_f)
            dve.tensor_copy(hw_v, hp_v)
            dve.tensor_copy(hw_g, hp_g)
            dve.drain()
            dve.sem_inc(sem("head_taken"), 1)

        def dve_level(dve, i, l):
            dve.wait_ge(sem("levels"), i * 8 + (l - 7))
            bank = psum[:, 2 + l % 2, :].rearrange("p (t s) -> p t s", t=LT)
            if l == 0:
                dve.tensor_tensor(hw_a, bank, bmid(masks[:, 0, :], LT), ALU.mult)
            else:
                h = 1 << (l - 1)
                f = hw_f[l - 1].rearrange("p d (n two) -> p d n two", two=2)
                dve.tensor_tensor(hw_f[l], f[:, :, :, 0], f[:, :, :, 1], ALU.mult)
                dve.copy_predicated(hw_a, bmid(masks[:, l, :], LT).bitcast(I32), bank)
                q = [hw_q[:, d, :].rearrange("p (n two h) -> p n two h", two=2, h=h) for d in range(2)]
                k = [hw_k[:, d, :].rearrange("p (n two h) -> p n two h", two=2, h=h) for d in range(2)]
                c0 = C // (2 * h)
                dve.tensor_tensor(q[1][:, :, 1, :], q[1][:, :, 1, :], bcast(f[:, 0, c0:, 0], h), ALU.mult)
                dve.tensor_tensor(q[0][:, :, 0, :], q[0][:, :, 0, :], bcast(f[:, 1, c0:, 1], h), ALU.mult)
                dve.tensor_tensor(k[0][:, :, 0, :], k[0][:, :, 0, :], bcast(f[:, 0, :, 1], h), ALU.mult)
                dve.tensor_tensor(k[1][:, :, 1, :], k[1][:, :, 1, :], bcast(f[:, 1, :, 0], h), ALU.mult)
            dve.drain()
            dve.sem_inc(sem("levels_out"), 1)

        def kt_bank(n):
            return psum[:, 4 + n // 4, (n % 4) * P:(n % 4 + 1) * P]

        def pe_turn_keys(pe, i):
            pe.wait_ge(sem("levels_out"), i * 8)
            pe.wait_ge(sem("head_out"), i)
            for n, (d, t) in enumerate([(0, t) for t in FWD_TILES] + [(1, t) for t in BWD_TILES]):
                mm = pe.transpose(kt_bank(n), hw_k[:, d, t * P:(t + 1) * P], ident)
            mm.then_inc(sem("keys_turned"), 1)

        def act_turn_keys(act, i):
            act.wait_ge(sem("keys_turned"), i)
            for b in range(3):
                m = 4 if b < 2 else 2
                ins = act.activation(hw_kt[:, 4 * b:4 * b + m, :],
                                     psum[:, 4 + b, 0:m * P].rearrange("p (a d) -> p a d", a=m), ACT.Copy)
            ins.then_inc(sem("keys_out"), 1)

        def pe_states(pe, i):
            pe.wait_ge(sem("keys_out"), i)
            for n, t in enumerate(FWD_TILES + BWD_TILES):
                mm = pe.matmul(kt_bank(n), hw_kt[:, n, :], hw_v[:, t, :], start=True, stop=True)
            mm.then_inc(sem("state_sums"), 1)

        def dve_states(dve, i):
            dve.wait_ge(sem("state_sums"), i)
            for m in range(5):
                for d, tiles in enumerate((FWD_TILES, BWD_TILES)):
                    n = 5 * d + m
                    if m == 0:
                        dve.tensor_copy(hw_s[:, n, :], kt_bank(n))
                    else:
                        dve.scalar_tensor_tensor(hw_s[:, n, :], hw_s[:, n - 1, :], hw_f[LEVELS][:, d, tiles[m]:tiles[m] + 1],
                                                 kt_bank(n), ALU.mult, ALU.add)
                dve.drain()
            dve.sem_inc(sem("states"), 1)

        def pe_outputs(pe, i):
            pe.wait_ge(sem("states"), i)
            for t in range(LT):
                o = psum[:, 7, t * P:(t + 1) * P]
                pe.matmul(o, hw_v[:, 2 + t, :], hw_a[:, t, :], start=True, stop=False)
                pe.matmul(o, hw_s[:, 1 + t, :], hw_q[:, 1, t * P:(t + 1) * P], start=False, stop=False)
                mm = pe.matmul(o, hw_s[:, 5 + 1 + (3 - t), :], hw_q[:, 0, t * P:(t + 1) * P], start=False, stop=True)
            mm.then_inc(sem("head_sums"), 1)

        def act_square(act, i):
            act.wait_ge(sem("head_sums"), i)
            act.activation(hw_sq, psum[:, 7, :], ACT.Square).then_inc(sem("head_squares"), 1)

        def pe_head_norm(pe, i):
            pe.wait_ge(sem("head_squares"), i)
            pe.matmul(psum[:, 4, :], ones, hw_sq, start=True, stop=True).then_inc(sem("head_mean"), 1)

        def act_root(act, i):
            act.wait_ge(sem("head_mean"), i)
            act.activation(hw_r, psum[:, 4, :], ACT.Sqrt, bias=eps, scale=1.0 / P).then_inc(sem("head_root"), 1)

        def dve_readout(dve, i):
            dve.wait_ge(sem("head_root"), i)
            dve.reciprocal(hw_r, hw_r)
            dve.drain()
            dve.tensor_tensor(hw_o, psum[:, 7, :], hw_r, ALU.mult)
            dve.drain()
            dve.scalar_tensor_tensor(aT[:, i - 1, :], hw_o, vec1[:, HGN:HGN + 8][:, bass.ds(i - 1, 1)], hw_g, ALU.mult, ALU.mult)
            dve.drain()
            dve.sem_inc(sem("head_out"), 1)

        def pe_hg(pe):
            pe.wait_ge(sem("normed"), n_lat + 1)
            for j in range(len(PIECES)):
                pe_piece(pe, 0, j)
            with pe.Fori(1, HEADS) as i:
                for j in range(len(PIECES)):
                    pe_piece(pe, i, j)
                    if j < 8:
                        pe_level(pe, i, j)
                    if j == 8:
                        pe_turn_keys(pe, i)
                    if j == 9:
                        pe_states(pe, i)
                    if j == 10:
                        pe_outputs(pe, i)
                        pe_head_norm(pe, i)
            for l in range(8):
                pe_level(pe, HEADS, l)
            for step in (pe_turn_keys, pe_states, pe_outputs, pe_head_norm):
                step(pe, HEADS)

        def act_hg(act):
            for j in ACT_PIECES:
                act_piece(act, 0, j)
            with act.Fori(1, HEADS) as i:
                for j in ACT_PIECES:
                    act_piece(act, i, j)
                    if j == 8:
                        act_turn_keys(act, i)
                act_square(act, i)
                act_root(act, i)
            for step in (act_turn_keys, act_square, act_root):
                step(act, HEADS)

        def dve_hg(dve):
            dve.sem_inc(sem("head_out"), 1)
            dve_conv1(dve, 0)
            dve_conv2(dve, 0)
            with dve.Fori(1, HEADS) as i:
                dve_take(dve, i)
                dve_level(dve, i, 0)
                dve_conv1(dve, i)
                dve_level(dve, i, 1)
                dve_conv2(dve, i)
                for l in range(2, 8):
                    dve_level(dve, i, l)
                dve_states(dve, i)
                dve_readout(dve, i)
            dve_take(dve, HEADS)
            for l in range(8):
                dve_level(dve, HEADS, l)
            dve_states(dve, HEADS)
            dve_readout(dve, HEADS)

        w_in64 = cut(A["w_in"][0], 64)

        def half_place(u, half):
            dst, lo_, hi_ = unit_place(u)
            return dst[:, :, 64 * half:64 * half + 64], lo_ + 512 * half, lo_ + 512 * half + 512

        ws.phase("attn", 4, [
            ((lambda i: w_in1[i * 2 + COL["aq"] // P]),) + unit_place(0),
            ((lambda i: w_in1[i * 2 + (COL["aq"] // P + 1)]),) + unit_place(1),
            ((lambda i: w_in64[i + COL["ak"] // 64]),) + half_place(2, 0),
            ((lambda i: w_in64[i + COL["ak"] // 64]),) + half_place(2, 1),
            ((lambda i: w_in64[i + COL["av"] // 64]),) + half_place(3, 0)])
        at = Carve(arena, CT_LO + 4096, UNIT_LO)
        ap_q = at.take(2, S)
        ap_k = at.take(T)
        ap_v = at.take(NT, 64)
        aw_q = at.take(4, S)
        aw_k = at.take(T)
        aw_v = at.take(NT, 64)
        ax_raw, ax_sq, ax_rt, ax_xn, ax_t = (at.take(S) for _ in range(5))
        a_prob = [at.take(T) for _ in range(2)]
        a_pt = [at.take(NT, S) for _ in range(2)]
        a_stat = at.take(4, 2)
        SCALE = 64 ** -0.5
        STEPS = 16
        AUX = [("proj", 0), ("sum", 0), ("rot", 0), ("proj", 1), ("sum", 1), ("rot", 1),
               ("klat", 2), ("sum", 2), ("rot", 2), ("kctx", 3), ("sum", 3), ("v", 4)]
        FIRST_ORDER = [0, 1, 3, 2, 4, 6, 5, 7, 9, 8, 10, 11]
        FIRST_BANK = {0: 2, 3: 3, 6: 4, 9: 5, 11: 6}

        def aux_mm(first):
            order = FIRST_ORDER if first else range(len(AUX))
            return [k for k in order if AUX[k][0] in ("sum", "rot", "klat")]

        def is_first(i):
            return isinstance(i, int) and i == 0

        def aux_bank(i, k):
            return FIRST_BANK.get(k, 0) if is_first(i) else 0

        AUX_MMS = 8
        AUX_ROOT = [k for k, (kind, _) in enumerate(AUX) if kind == "sum"]
        NAUX = len(AUX)

        def aux_n(item):
            return C if item == 3 else S

        def aux_done(eng, i, k):
            if k in aux_mm(False):
                eng.wait_ge(sem("aux_product"), i * AUX_MMS + (aux_mm(is_first(i)).index(k) + 1))
            else:
                unit = {0: 0, 3: 1, 9: 3, 11: 4}[k]
                eng.wait_ge(sem("weights_used"), i * 5 + (ws.phases["attn"]["base"] + unit + 1))

        def pe_aux(pe, i, k):
            kind, item = AUX[k]
            if not (is_first(i) and k in FIRST_BANK):
                wait(pe, sem("aux_out"), i * NAUX + k)
            bank = psum[:, aux_bank(i, k), :]
            n = aux_n(item)
            if kind in ("proj", "klat", "kctx"):
                if kind == "proj":
                    ws.arrived(pe, "attn", i, item)
                if kind == "klat":
                    ws.arrived(pe, "attn", i, 2)
                    ws.arrived(pe, "attn", i, 3)
                w = unit_place(min(item, 2))[0]
                x = HT[:, :, 0:C] if kind == "kctx" else HT[:, :, C:T]
                for c in range(KC):
                    mm = pe.matmul(bank[:, 0:n], w[:, c, :], x[:, c, :], start=(c == 0), stop=(c == KC - 1))
                if kind == "klat":
                    mm.then_inc(sem("aux_product"), 1)
                else:
                    mm.then_inc(sem("weights_used"), 2 if kind == "kctx" else 1)
            elif kind == "v":
                ws.arrived(pe, "attn", i, 4)
                w = ws.dst("attn", 4)
                for t in range(NT):
                    for c in range(KC):
                        mm = pe.matmul(bank[:, 64 * t:64 * t + 64], HT[:, c, t * P:(t + 1) * P], w[:, c, :],
                                       start=(c == 0), stop=(c == KC - 1))
                mm.then_inc(sem("weights_used"), 1)
            elif kind == "sum":
                pe.matmul(bank[:, 0:n], ones_half, ax_sq[:, 0:n], start=True, stop=True).then_inc(sem("aux_product"), 1)
            else:
                pe.matmul(bank, rot, ax_xn, start=True, stop=True).then_inc(sem("aux_product"), 1)

        def act_aux(act, i, k):
            kind, item = AUX[k]
            n = aux_n(item)
            bank = psum[:, aux_bank(i, k), 0:n]
            if kind == "rot":
                return
            aux_done(act, i, k)
            if is_first(i) and k in FIRST_BANK:
                wait(act, sem("aux_out"), k)
            if kind in ("proj", "klat", "kctx"):
                act.activation(ax_raw[:, 0:n], bank, ACT.Copy)
                act.activation(ax_sq[:, 0:n], bank, ACT.Square).then_inc(sem("aux_out"), 1)
            elif kind == "v":
                wait(act, sem("attn_taken"), i * 2)
                act.activation(ap_v, psum[:, aux_bank(i, k), 0:NT * 64].rearrange("p (t e) -> p t e", t=NT), ACT.Copy)\
                   .then_inc(sem("aux_out"), 1)
            else:
                act.activation(ax_rt[:, 0:n], bank, ACT.Sqrt, bias=eps, scale=1.0 / 64).then_inc(sem("aux_root"), 1)

        def dve_aux(dve, i, k):
            kind, item = AUX[k]
            n = aux_n(item)
            if kind == "sum":
                dve.wait_ge(sem("aux_root"), i * 4 + (AUX_ROOT.index(k) + 1))
                dve.reciprocal(ax_rt[:, 0:n], ax_rt[:, 0:n])
                dve.drain()
                g = vec1[:, QN:QN + 1] if item < 2 else vec1[:, KN:KN + 1]
                dst = ap_k[:, 0:C] if item == 3 else ax_xn
                dve.scalar_tensor_tensor(dst, ax_raw[:, 0:n], g, ax_rt[:, 0:n], ALU.mult, ALU.mult)
                dve.drain()
                dve.sem_inc(sem("aux_out"), 1)
            if kind == "rot":
                aux_done(dve, i, k)
                dve.tensor_tensor(ax_t, psum[:, 0, :], sin, ALU.mult)
                dve.tensor_tensor(ax_xn, ax_xn, cos, ALU.mult)
                dve.drain()
                dve.tensor_tensor(ap_k[:, C:T] if item == 2 else ap_q[:, item, :], ax_xn, ax_t, ALU.add)
                dve.drain()
                dve.sem_inc(sem("aux_out"), 1)

        def earlier(i, n, needed):
            return n >= needed or not (isinstance(i, int) and i == 1)

        def at_step(i, s):
            return (i - 1) * STEPS + s if isinstance(i, int) else i * STEPS + (s - STEPS)

        def score_banks(s):
            return psum[:, 2 + 2 * (s % 2):4 + 2 * (s % 2), :].rearrange("p b n -> p (b n)")[:, 0:T]

        def pe_scores(pe, i, s):
            j, t = s // 4, s % 4
            if s == 0:
                pe.wait_ge(sem("attn_taken"), i * 2 - 1)
            if earlier(i, s, 2):
                pe.wait_ge(sem("exps"), at_step(i, s - 1))
            q = aw_q[:, j, t * P:(t + 1) * P]
            o = score_banks(s)
            pe.matmul(o[:, 0:BANK], q, aw_k[:, 0:BANK], start=True, stop=True)
            pe.matmul(o[:, BANK:T], q, aw_k[:, BANK:T], start=True, stop=True).then_inc(sem("scores"), 1)

        def dve_max(dve, i, s):
            dve.wait_ge(sem("scores"), at_step(i, s + 1))
            dve.tensor_reduce(a_stat[:, s % 2, 0:1], score_banks(s), AX, ALU.max)
            dve.drain()
            dve.tensor_scalar(a_stat[:, s % 2, 1:2], a_stat[:, s % 2, 0:1], -SCALE, None, ALU.mult)\
               .then_inc(sem("row_max"), 1)

        def act_exp(act, i, s):
            act.wait_ge(sem("row_max"), at_step(i, s + 1))
            if earlier(i, s, 2):
                act.wait_ge(sem("probs_turned"), at_step(i, s - 1))
            act.activation(a_prob[s % 2], score_banks(s), ACT.Exp, bias=a_stat[:, s % 2, 1:2], scale=SCALE,
                           accum_out=a_stat[:, 2 + s % 2, 0:1]).then_inc(sem("exps"), 1)

        def dve_scale(dve, i, s):
            dve.wait_ge(sem("exps"), at_step(i, s + 1))
            dve.reciprocal(a_stat[:, 2 + s % 2, 1:2], a_stat[:, 2 + s % 2, 0:1])
            dve.drain()
            dve.tensor_scalar(a_prob[s % 2], a_prob[s % 2], a_stat[:, 2 + s % 2, 1:2], None, ALU.mult)\
               .then_inc(sem("probs"), 1)

        def pe_turn_probs(pe, i, s):
            pe.wait_ge(sem("probs"), at_step(i, s + 1))
            if earlier(i, s, 1):
                pe.wait_ge(sem("probs_out"), at_step(i, s))
            o = psum[:, 6:8, :].rearrange("p b n -> p (b n)")
            for t in range(NT):
                mm = pe.transpose(o[:, t * P:(t + 1) * P], a_prob[s % 2][:, t * P:(t + 1) * P], ident)
            mm.then_inc(sem("probs_turned"), 1)

        def act_turn_probs(act, i, s):
            j, t = s // 4, s % 4
            act.wait_ge(sem("probs_turned"), at_step(i, s + 1))
            if t == 0 and earlier(i, j, 2):
                act.wait_ge(sem("weighted"), i * 4 + (j - 1 - 4))
            o = psum[:, 6:8, :].rearrange("p b n -> p (b n)")[:, 0:T].rearrange("p (a n) -> p a n", a=NT)
            act.activation(a_pt[j % 2][:, :, t * P:(t + 1) * P], o, ACT.Copy).then_inc(sem("probs_out"), 1)

        def pe_values(pe, i, j):
            pe.wait_ge(sem("probs_out"), at_step(i, 4 * j + 4))
            if j == 0:
                pe.wait_ge(sem("attn_taken"), i * 2)
            pe.wait_ge(sem("attended"), i * 4 + (j + 1 - 4))
            h = 64 * (j % 2)
            for t in range(NT):
                mm = pe.matmul(psum[h:h + 64, 1, :], aw_v[:, t, :], a_pt[j % 2][:, t, :], start=(t == 0), stop=(t == NT - 1))
            mm.then_inc(sem("weighted"), 1)

        def act_values(act, i, j):
            act.wait_ge(sem("weighted"), i * 4 + (j + 1 - 4))
            h = 64 * (j % 2)
            act.activation(cT[h:h + 64, i * 2 + (j // 2 - 2), :], psum[h:h + 64, 1, :], ACT.Copy).then_inc(sem("attended"), 1)

        def dve_attn_take(dve, i):
            dve.wait_ge(sem("aux_out"), i * NAUX)
            for half in range(2):
                rows = slice(64 * half, 64 * half + 64)
                dve.tensor_copy(aw_q.rearrange("p (c two) n -> p two c n", two=2)[rows, half], ap_q[rows])
            dve.tensor_copy(aw_k, ap_k)
            dve.drain()
            dve.sem_inc(sem("attn_taken"), 1)

        def dve_values_take(dve, i):
            dve.wait_ge(sem("attended"), i * 4 - 3)
            dve.tensor_copy(aw_v, ap_v).then_inc(sem("attn_taken"), 1)

        def before(i, s, back):
            if s >= back:
                return i, s - back
            return (i - 1, s - back + STEPS) if earlier(i, s, back) else None

        def pe_attn_iter(pe, i, aux):
            for s in range(STEPS):
                pe_scores(pe, i, s)
                pe_attn_rest(pe, before(i, s, 2), lambda: aux and s < NAUX and pe_aux(pe, i, s))

        def pe_attn_rest(pe, step, aux):
            if step:
                pe_turn_probs(pe, *step)
            aux()
            if step and step[1] % 4 == 0 and before(*step, 4):
                j, s = before(*step, 4)
                pe_values(pe, j, s // 4)

        def act_attn_iter(act, i, aux):
            for s in range(STEPS):
                act_exp(act, i, s)
                act_attn_rest(act, before(i, s, 2), lambda: aux and s < NAUX and act_aux(act, i, s))

        def act_attn_rest(act, step, aux):
            if step:
                act_turn_probs(act, *step)
            aux()
            if step and step[1] % 4 == 0 and before(*step, 4):
                j, s = before(*step, 4)
                act_values(act, j, s // 4)

        def dve_attn_iter(dve, i, aux):
            dve_attn_take(dve, i)
            for s in range(STEPS):
                dve_max(dve, i, s)
                if before(i, s, 1):
                    dve_scale(dve, *before(i, s, 1))
                if s == 4:
                    dve_values_take(dve, i)
                if aux and s < NAUX:
                    dve_aux(dve, i, s)

        def pe_attn(pe):
            pe.wait_ge(sem("head_out"), HEADS + 1)
            for k in FIRST_ORDER:
                pe_aux(pe, 0, k)
            pe_attn_iter(pe, 1, True)
            with pe.Fori(2, 4) as i:
                pe_attn_iter(pe, i, True)
            pe_attn_iter(pe, 4, False)
            for s in (STEPS - 2, STEPS - 1):
                pe_turn_probs(pe, 4, s)
            pe_values(pe, 4, 3)

        def act_attn(act):
            act.wait_ge(sem("head_out"), HEADS + 1)
            act.sem_inc(sem("attended"), 1)
            for k in range(NAUX):
                act_aux(act, 0, k)
            act_attn_iter(act, 1, True)
            with act.Fori(2, 4) as i:
                act_attn_iter(act, i, True)
            act_attn_iter(act, 4, False)
            for s in (STEPS - 2, STEPS - 1):
                act_turn_probs(act, 4, s)
            act_values(act, 4, 3)

        def dve_attn(dve):
            dve.memset(aw_q, 0.0)
            dve.drain()
            for k in range(NAUX):
                dve_aux(dve, 0, k)
            dve_attn_iter(dve, 1, True)
            with dve.Fori(2, 4) as i:
                dve_attn_iter(dve, i, True)
            dve_attn_iter(dve, 4, False)
            dve_scale(dve, 4, STEPS - 1)

        w_proj = [cut(A[n][0], P) for n in ("w_proj_a", "w_proj_b", "w_proj_c")]
        units = []
        for b in range(3):
            units.append(((lambda i, b=b: w_in1[i + COL["g" + "abc"[b]] // P]),) + unit_place(2 * b))
            units.append(((lambda i, b=b: w_proj[b][i]),) + unit_place(2 * b + 1))
        ws.phase("merge", KC, units)
        mg = Carve(arena, EXTRA[0], UNIT_LO)
        m_gate = [mg.take(S) for _ in range(3)]
        m_t = mg.take(S)
        branches = [aT, bT, cT]

        def done(eng, name, i, u):
            ph = ws.phases[name]
            eng.wait_ge(sem("weights_used"), i * len(ph["units"]) + (ph["base"] + u + 1))

        def pe_merge(pe):
            pe.wait_ge(sem("attended"), 17)
            with pe.Fori(0, KC) as i:
                for b in range(3):
                    for u, x, bank, s in ((2 * b, HT[:, :, C:T], b, "gate_out"), (2 * b + 1, branches[b], 3 + b, "branch_out")):
                        ws.arrived(pe, "merge", i, u)
                        pe.wait_ge(sem(s), i * 3 + (b + 1))
                        for k in range(KC):
                            mm = pe.matmul(psum[:, bank, :], ws.dst("merge", u)[:, k, :], x[:, k, :],
                                           start=(k == 0), stop=(k == KC - 1))
                        mm.then_inc(sem("weights_used"), 1)

        def act_merge(act):
            act.sem_inc(sem("gate_out"), 3)
            with act.Fori(0, KC) as i:
                for b in range(3):
                    done(act, "merge", i, 2 * b)
                    act.wait_ge(sem("branch_out"), i * 3 + (b + 1))
                    act.activation(m_gate[b], psum[:, b, :], ACT.Sigmoid).then_inc(sem("gate_out"), 1)

        def dve_merge(dve):
            dve.sem_inc(sem("branch_out"), 3)
            with dve.Fori(0, KC) as i:
                for b in range(3):
                    done(dve, "merge", i, 2 * b + 1)
                    dve.wait_ge(sem("gate_out"), i * 3 + (b + 4))
                    dve.tensor_tensor(m_t if b else yT[:, i, :], m_gate[b], psum[:, 3 + b, :], ALU.mult)
                    dve.drain()
                    dve.sem_inc(sem("branch_out"), 1)
                    if b:
                        dve.tensor_tensor(yT[:, i, :], yT[:, i, :], m_t, ALU.add)
                        dve.drain()
            dve.sem_inc(sem("merged"), 1)

        def residual(name, iters, units, x, out_fn, first=(), places=None):
            ws.phase(name, iters, units, places)
            n = len(units)

            def pe_part(pe):
                for s, v in first:
                    pe.wait_ge(sem(s), v)
                with pe.Fori(0, iters) as i:
                    for u in range(n):
                        ws.arrived(pe, name, i, u)
                        pe.wait_ge(sem(name + "_out"), i * n + (u + 1))
                        for k in range(KC):
                            mm = pe.matmul(psum[:, u % 4, :], ws.dst(name, u)[:, k, :], x[:, k, :],
                                           start=(k == 0), stop=(k == KC - 1))
                        mm.then_inc(sem("weights_used"), 1)

            def dve_part(dve):
                dve.sem_inc(sem(name + "_out"), n)
                with dve.Fori(0, iters) as i:
                    for u in range(n):
                        done(dve, name, i, u)
                        out_fn(dve, i * n + u, psum[:, u % 4, :]).then_inc(sem(name + "_out"), 1)
                dve.drain()
                dve.sem_inc(sem(name + "_done"), 1)
            return pe_part, dve_part

        def add_gated(gain):
            def fn(dve, c, bank):
                return dve.scalar_tensor_tensor(XT[:, c, :], bank, gain[:, bass.ds(c, 1)], XT[:, c, :], ALU.mult, ALU.add)
            return fn

        w_out1 = cut(A["w_out"][0], P)
        g_a = fix.take(KC)
        g_f = fix.take(KC)
        pe_wout, dve_wout = residual("w_out", 2, [((lambda i, u=u: w_out1[i * 4 + u]),) + unit_place(v) for u, v in enumerate((6, 7, 0, 1))],
                                     yT, add_gated(g_a), (("merged", 1),), [6, 7, 0, 1])

        def dve_gains(dve):
            dve.tensor_copy(g_a, mod[:, G_A * KC:G_A * KC + KC, 0])
            dve.tensor_copy(g_f, mod[:, G_F * KC:G_F * KC + KC, 0])
            dve.drain()

        h2T = Carve(arena, HT_LO, HT_LO + 4096).take(KC, S)
        n_ffn = norm(XT, h2T, S, lambda k: scale2[:, k:k + 1], lambda k: mod[:, SH_F * KC + k, 0:1], 4,
                     Carve(arena, EXTRA[0], EXTRA[1]).take(S), before=(("w_out_done", 1),))
        h2tok = yT.rearrange("p k n -> p (k n)").rearrange("p (t d) -> p t d", t=LT)
        hot = cT.rearrange("p k n -> p (k n)").rearrange("p (t e c) -> p t e c", t=LT, e=NE)
        xsT = Carve(arena, BT_LO, CT_LO).take(KC, NE * CAP)
        whot = Carve(arena, HT_LO, HT_LO + 4096).take(LT, NE, CAP)
        turned_hot = Carve(arena, EXTRA[0], EXTRA[0] + 4096).take(KC, S)
        rt = Carve(arena, EXTRA[0] + 4096, RING_LO)
        router = rt.take(KC, NE)
        aff = rt.take(LT, NE)
        aff_st = rt.take(LT, 2)
        slotT = rt.take(LT, NE)
        rr = Carve(arena, HT_LO + 4096, HT_LO + 6144)
        aff_row, row_work, row_a, row_b = (rr.take(S) for _ in range(4))
        top8 = rt.take(8, 8)

        def sp_router(sp):
            sp.dma_start(router, A["router_w"][0].rearrange("(k p) e -> p k e", p=P)).then_inc(sem("router_in"), 16)

        def pe_router(pe):
            pe.wait_ge(sem("router_in"), 16)
            pe.wait_ge(sem("normed"), n_ffn + 1)
            for t in range(LT):
                for k in range(KC):
                    mm = pe.matmul(psum[:, 5, t * NE:(t + 1) * NE], h2T[:, k, t * P:(t + 1) * P], router[:, k, :],
                                   start=(k == 0), stop=(k == KC - 1))
            mm.then_inc(sem("logits"), 1)
            for n in range(8):
                if n >= 4:
                    pe.wait_ge(sem("htok_out"), n - 3)
                for c in range(4):
                    mm = pe.transpose(psum[:, n % 4, c * P:(c + 1) * P],
                                      h2T[:, 4 * (n % 2) + c, (n // 2) * P:(n // 2 + 1) * P], ident)
                mm.then_inc(sem("htok"), 1)
            pe.wait_ge(sem("affinity"), 1)
            for t in range(LT):
                mm = pe.transpose(psum[0:NE, 6, t * P:(t + 1) * P], aff[:, t, :], ident)
            mm.then_inc(sem("aff_turned"), 1)
            pe.wait_ge(sem("slots_row"), 1)
            for t in range(LT):
                mm = pe.transpose(psum[:, 7, t * NE:(t + 1) * NE], row_a[0:NE, t * P:(t + 1) * P], ident[0:NE, 0:NE])
            mm.then_inc(sem("slots_turned"), 1)

        def act_router(act):
            for n in range(8):
                act.wait_ge(sem("htok"), n + 1)
                act.activation(h2tok[:, n // 2, (n % 2) * 512:(n % 2) * 512 + 512], psum[:, n % 4, :], ACT.Copy)\
                   .then_inc(sem("htok_out"), 1)
                if n == 0:
                    act.wait_ge(sem("logits_shifted"), 1)
                    act.activation(aff, aff, ACT.Exp).then_inc(sem("aff_exp"), 1)

        def dve_router(dve):
            dve.wait_ge(sem("logits"), 1)
            lg = psum[:, 5, 0:LT * NE].rearrange("p (t e) -> p t e", t=LT)
            dve.tensor_reduce(aff_st[:, :, 0], lg, AX, ALU.max)
            dve.drain()
            dve.tensor_tensor(aff, lg, bcast(aff_st[:, :, 0], NE), ALU.subtract)
            dve.drain()
            dve.sem_inc(sem("logits_shifted"), 1)
            dve.wait_ge(sem("aff_exp"), 1)
            dve.tensor_reduce(aff_st[:, :, 0], aff, AX, ALU.add)
            dve.drain()
            dve.reciprocal(aff_st[:, :, 1], aff_st[:, :, 0])
            dve.drain()
            dve.tensor_tensor(aff, aff, bcast(aff_st[:, :, 1], NE), ALU.mult)
            dve.drain()
            dve.sem_inc(sem("affinity"), 1)
            dve.wait_ge(sem("aff_turned"), 1)
            work = [row_work[0:NE, :], row_b[0:NE, :]]
            dve.tensor_copy(work[0], psum[0:NE, 6, :])
            dve.drain()
            for r in range(CAP // 8):
                dve.max(top8[0:NE, r, :], work[r % 2])
                dve.drain()
                dve.match_replace(work[(r + 1) % 2], top8[0:NE, r, :], work[r % 2], -1.0)
                dve.drain()
            chosen = row_b[0:NE, :]
            dve.tensor_scalar(chosen, work[0], 0.0, None, ALU.is_lt)
            dve.drain()
            dve.tensor_tensor_scan(row_work[0:NE, :], chosen, chosen, 0.0, ALU.add, ALU.max)
            dve.drain()
            dve.tensor_tensor(row_work[0:NE, :], row_work[0:NE, :], chosen, ALU.mult)
            dve.drain()
            dve.tensor_scalar(row_a[0:NE, :], row_work[0:NE, :], 1.0, None, ALU.subtract).then_inc(sem("slots_row"), 1)
            dve.wait_ge(sem("slots_turned"), 1)
            dve.tensor_copy(slotT, psum[:, 7, 0:LT * NE].rearrange("p (t e) -> p t e", t=LT))
            dve.drain()
            for t in range(LT):
                dve.tensor_tensor(hot[:, t], bmid(slots, NE), bcast(slotT[:, t, :], CAP), ALU.is_equal)
            dve.drain()
            dve.sem_inc(sem("one_hot"), 1)
            for t in range(LT):
                dve.tensor_tensor(whot[:, t], hot[:, t], bcast(aff[:, t, :], CAP), ALU.mult)
            dve.drain()
            dve.sem_inc(sem("weighted_hot"), 1)

        def pe_gather(pe):
            pe.wait_ge(sem("one_hot"), 1)
            pe.wait_ge(sem("htok_out"), 8)
            n = 0
            for k in range(KC):
                for half in range(2):
                    if n >= 4:
                        pe.wait_ge(sem("gather_out"), n - 3)
                    for t in range(LT):
                        mm = pe.matmul(psum[:, n % 4, :], h2tok[:, t, k * P:(k + 1) * P],
                                       hot[:, t].rearrange("p e c -> p (e c)")[:, half * 512:half * 512 + 512],
                                       start=(t == 0), stop=(t == LT - 1))
                    mm.then_inc(sem("gathered"), 1)
                    n += 1
            pe.wait_ge(sem("weighted_hot"), 1)
            for pair in range(NE // 2):
                if pair >= 2:
                    pe.wait_ge(sem("hot_out"), pair - 1)
                for t in range(LT):
                    mm = pe.transpose(psum[:, 6 + pair % 2, t * P:(t + 1) * P],
                                      whot[:, t].rearrange("p e c -> p (e c)")[:, pair * P:(pair + 1) * P], ident)
                mm.then_inc(sem("hot_turned"), 1)

        def act_gather(act):
            for n in range(16):
                act.wait_ge(sem("gathered"), n + 1)
                act.activation(xsT[:, n // 2, (n % 2) * 512:(n % 2) * 512 + 512], psum[:, n % 4, :], ACT.Copy)\
                   .then_inc(sem("gather_out"), 1)

        def dve_gather(dve):
            for pair in range(NE // 2):
                dve.wait_ge(sem("hot_turned"), pair + 1)
                dve.tensor_copy(turned_hot[:, pair, :], psum[:, 6 + pair % 2, :]).then_inc(sem("hot_out"), 1)

        wg = A["w_gate"][0].rearrange("(i e) (k p) (c n) -> i e c p k n", e=2, p=P, n=512)
        wu = A["w_up"][0].rearrange("(i e) (k p) (c n) -> i e c p k n", e=2, p=P, n=512)
        wd = A["w_down"][0].rearrange("(i e) (k p) (c n) -> i e c p k n", e=2, p=P, n=512)
        units, slot_of = [], []
        for e in range(2):
            for n, (w, c) in enumerate([(wg, 0), (wu, 0), (wg, 1), (wu, 1), (wd, 0), (wd, 1)]):
                q = (6 * e + n) % 4
                units.append(((lambda i, w=w, c=c, e=e: w[i, e, c]),) + quad_place(q))
                slot_of.append(q)
        ws.phase("experts", NE // 2, units, slot_of)
        ys = Carve(arena, CT_LO, CT_LO + 8192).take(NE // 2, D)
        ex = Carve(arena, HT_LO, HT_LO + 6144)
        xs = [ex.take(KC, CAP) for _ in range(2)]
        e_gate = [ex.take(S) for _ in range(2)]
        e_hid = [ex.take(S) for _ in range(2)]
        e_hidT = [ex.take(4, CAP) for _ in range(2)]
        xs_all = xsT.rearrange("p k (i e c) -> p k i e c", e=2, c=CAP)

        def blocks(e):
            return {name: 6 * e + n for n, name in enumerate(["g0", "u0", "g1", "u1", "d0", "d1"])}

        def pe_experts(pe):
            pe.wait_ge(sem("hot_out"), NE // 2)
            pe.wait_ge(sem("gather_out"), 16)
            with pe.Fori(0, NE // 2) as i:
                for e in range(2):
                    b = blocks(e)
                    pe.wait_ge(sem("expert_tokens"), i * 2 + (e + 1))
                    pe.wait_ge(sem("ys_out"), i * 2 + (e + 1))

                    def into(bank, name):
                        ws.arrived(pe, "experts", i, b[name])
                        for k in range(KC):
                            mm = pe.matmul(psum[0:CAP, bank, :], xs[e][:, k, :], ws.dst("experts", b[name])[:, k, :],
                                           start=(k == 0), stop=(k == KC - 1))
                        mm.then_inc(sem("weights_used"), 1)

                    def turn(half):
                        pe.wait_ge(sem("hidden"), i * 4 + (2 * e + half + 1))
                        o = psum[:, 4 + 3 * half, 0:4 * CAP]
                        for c in range(4):
                            src = e_hid[half][0:CAP, c * P:(c + 1) * P]
                            if c == 0:
                                pe.matmul(o[:, 0:CAP], src, ident[0:CAP, 0:CAP], start=True, stop=True)
                            else:
                                mm = pe.transpose(o[:, c * CAP:(c + 1) * CAP], src, ident[0:CAP, 0:CAP])
                        mm.then_inc(sem("hidden_turned"), 1)

                    def down(half, n):
                        if half == 0:
                            ws.arrived(pe, "experts", i, b[f"d{n}"])
                        pe.wait_ge(sem("hidden_out"), i * 4 + (2 * e + half + 1))
                        for c in range(4):
                            mm = pe.matmul(psum[64 * e:64 * e + 64, 5 + n, :], e_hidT[half][:, c, :],
                                           ws.dst("experts", b[f"d{n}"])[:, 4 * half + c, :],
                                           start=(half == 0 and c == 0), stop=(half == 1 and c == 3))
                        if half == 1:
                            mm.then_inc(sem("weights_used"), 1)

                    into(0, "g0")
                    into(2, "u0")
                    into(1, "g1")
                    turn(0)
                    into(3, "u1")
                    down(0, 0)
                    turn(1)
                    down(0, 1)
                    down(1, 0)
                    down(1, 1)

        def act_experts(act):
            act.sem_inc(sem("ys_out"), 1)
            with act.Fori(0, NE // 2) as i:
                for e in range(2):
                    b = blocks(e)
                    for half in range(2):
                        done(act, "experts", i, b[f"g{half}"])
                        act.activation(e_gate[half][0:CAP, :], psum[0:CAP, half, :], ACT.Silu).then_inc(sem("expert_silu"), 1)
                        if half == 1:
                            turn_out(act, i, e, 0)
                    turn_out(act, i, e, 1)
                    done(act, "experts", i, b["d1"])
                    act.activation(ys[64 * e:64 * e + 64, i, :], psum[64 * e:64 * e + 64, 5:7, :].rearrange("p b n -> p (b n)"),
                                   ACT.Copy).then_inc(sem("ys_out"), 1)

        def turn_out(act, i, e, half):
            act.wait_ge(sem("hidden_turned"), i * 4 + (2 * e + half + 1))
            act.activation(e_hidT[half], psum[:, 4 + 3 * half, 0:4 * CAP].rearrange("p (c t) -> p c t", c=4), ACT.Copy)\
               .then_inc(sem("hidden_out"), 1)

        def dve_experts(dve):
            dve.wait_ge(sem("gather_out"), 16)
            with dve.Fori(0, NE // 2) as i:
                for e in range(2):
                    b = blocks(e)
                    dve.wait_ge(sem("weights_used"), i * 12 + (ws.phases["experts"]["base"] + b["u1"] + 1 - 12))
                    dve.tensor_copy(xs[e], xs_all[:, :, i, e, :]).then_inc(sem("expert_tokens"), 1)
                    for half in range(2):
                        dve.wait_ge(sem("expert_silu"), i * 4 + (2 * e + half + 1))
                        done(dve, "experts", i, b[f"u{half}"])
                        dve.tensor_tensor(e_hid[half][0:CAP, :], e_gate[half][0:CAP, :], psum[0:CAP, 2 + half, :], ALU.mult)\
                           .then_inc(sem("hidden"), 1)

        def pe_scatter(pe):
            pe.wait_ge(sem("ys_out"), NE + 1)
            for n in range(KC):
                if n >= 4:
                    pe.wait_ge(sem("scatter_out"), n - 3)
                for pair in range(NE // 2):
                    mm = pe.matmul(psum[:, n % 4, :], ys[:, pair, n * P:(n + 1) * P], turned_hot[:, pair, :],
                                   start=(pair == 0), stop=(pair == NE // 2 - 1))
                mm.then_inc(sem("scattered"), 1)

        def dve_scatter(dve):
            for n in range(KC):
                dve.wait_ge(sem("scattered"), n + 1)
                dve.scalar_tensor_tensor(XT[:, n, :], psum[:, n % 4, :], g_f[:, n:n + 1], XT[:, n, :], ALU.mult, ALU.add)\
                   .then_inc(sem("scatter_out"), 1)

        X2 = Carve(arena, HT_LO, HT_LO + 4096).take(KC, S)
        n_fin1 = norm(XT, X2, S, lambda k: vec1[:, FIN1 + k:FIN1 + k + 1], None, 4,
                      Carve(arena, HT_LO + 4096, HT_LO + 6144).take(S), before=(("scatter_out", KC),))

        hm = bT
        n_mix = norm(X2, hm, S, lambda k: vec2[:, MIXN + k:MIXN + k + 1], None, 4,
                     Carve(arena, HT_LO + 4096, HT_LO + 6144).take(S), before=(("normed", n_fin1 + 1),))
        w_in2 = A["w_in_2"][0][:, 0:2560].rearrange("(k p) (c n) -> c p k n", p=P, n=P)
        POOL_COL, QKV_COL, Z_COL = 0, 4, 16
        ws.phase("pool2", 1, [((lambda i, u=u: w_in2[POOL_COL + u]),) + unit_place(u) for u in range(4)])
        ws.phase("qkv2", 3, [((lambda i, u=u: w_in2[i * 4 + (QKV_COL + u)]),) + unit_place(4 + u) for u in range(4)], [4, 5, 6, 7])
        ws.phase("z2", 1, [((lambda i, u=u: w_in2[Z_COL + u]),) + unit_place(u) for u in range(4)])
        ydT = aT
        qkv = Carve(arena, CT_LO, CT_LO + 6144).take(12, S)
        z_silu = Carve(arena, CT_LO + 6144, CT_LO + 8192).take(DNH, S)
        dn = Carve(arena, EXTRA[0], UNIT_LO)
        w_ba = dn.take(KC, 8)
        head_par = dn.take(2)
        row_b, row_g, row_t, row_e, row_c = (dn.take(S) for _ in range(5))
        DN_LO = dn.at
        w_pool = dn.take(4, P)
        counts = dn.take(4, S)
        p_u = dn.take(S)
        p_s = [dn.take(S) for _ in range(2)]
        p_mix = [dn.take(S) for _ in range(4)]
        cv_x = [dn.take(S) for _ in range(2)]
        cv_w = [dn.take(S) for _ in range(2)]

        def sp_small2(sp):
            sp.wait_ge(sem("normed"), n_fin1 + 1)
            sp.dma_start(w_ba, A["w_in_2"][0][:, 2560:2568].rearrange("(k p) n -> p k n", p=P)).then_inc(sem("small2"), 16)
            sp.dma_start(w_pool, A["w_pool_2"][0].rearrange("g c d -> c g d")).then_inc(sem("small2"), 16)
            at_, n_ = CONST_COLS["counts"]
            sp.dma_start(counts.rearrange("p a b -> p (a b)"), A["const_table"][:, at_:at_ + n_]).then_inc(sem("small2"), 16)
            sp.dma_start(head_par[0:DNH, 0:1], A["a_log_2"].rearrange("l h -> h l")).then_inc(sem("small2"), 16)
            sp.dma_start(head_par[0:DNH, 1:2], A["dt_bias_2"].rearrange("l h -> h l")).then_inc(sem("small2"), 16)

        def product(pe, name, i, u, x, bank, n=S):
            ws.arrived(pe, name, i, u)
            w = ws.dst(name, u)
            for k in range(KC):
                mm = pe.matmul(psum[:, bank, 0:n], w[:, k, :], x[:, k, :], start=(k == 0), stop=(k == KC - 1))
            mm.then_inc(sem("weights_used"), 1)

        def pe_in2(pe):
            pe.wait_ge(sem("small2"), 80)
            pe.wait_ge(sem("normed"), n_mix + 1)
            for m in range(2):
                for k in range(KC):
                    mm = pe.matmul(psum[0:DNH, 6 + m, :], w_ba[:, k, 4 * m:4 * m + 4], hm[:, k, :],
                                   start=(k == 0), stop=(k == KC - 1))
            mm.then_inc(sem("rows2"), 1)
            for g in range(4):
                if g >= 2:
                    mix_pool(pe, g - 2)
                product(pe, "pool2", 0, g, hm, g % 2)
            with pe.Fori(0, 3) as i:
                for u in range(4):
                    pe.wait_ge(sem("qkv_out"), i * 4 + (u + 1))
                    product(pe, "qkv2", i, u, hm, 2 + u % 2)
            for g in (2, 3):
                pe.wait_ge(sem("pool_out"), g - 1)
                mix_pool(pe, g)
            for u in range(4):
                if u >= 2:
                    pe.wait_ge(sem("z_out"), u - 1)
                product(pe, "z2", 0, u, hm, u % 2)

        def mix_pool(pe, g):
            pe.wait_ge(sem("pooled"), g + 1)
            pe.matmul(psum[:, 4 + g % 2, :], w_pool[:, g, :], p_mix[g], start=True, stop=True).then_inc(sem("pool_mixed"), 1)

        def act_in2(act):
            act.wait_ge(sem("small2"), 80)
            act.sem_inc(sem("qkv_out"), 2)
            act.sem_inc(sem("qkv_silu"), 2)
            act.wait_ge(sem("rows2"), 1)
            act.activation(row_b[0:DNH, :], psum[0:DNH, 6, :], ACT.Sigmoid)
            act.activation(row_t[0:DNH, :], psum[0:DNH, 7, :], ACT.Identity, bias=head_par[0:DNH, 1:2]).then_inc(sem("dt_added"), 1)
            act.activation(head_par[0:DNH, 0:1], head_par[0:DNH, 0:1], ACT.Exp).then_inc(sem("dt_added"), 1)
            act.drain()
            act.activation(row_e[0:DNH, :], row_t[0:DNH, :], ACT.Abs)
            act.drain()
            act.activation(row_e[0:DNH, :], row_e[0:DNH, :], ACT.Exp, scale=-1.0)
            act.drain()
            act.activation(row_e[0:DNH, :], row_e[0:DNH, :], ACT.Ln, bias=ones[0:DNH, 0:1]).then_inc(sem("row_ln"), 1)
            with act.Fori(0, 3) as i:
                for u in range(4):
                    act.wait_ge(sem("weights_used"), i * 4 + (ws.phases["qkv2"]["base"] + u + 1))
                    act.activation(cv_x[u % 2], psum[:, 2 + u % 2, :], ACT.Copy).then_inc(sem("qkv_out"), 1)
                    act.wait_ge(sem("conv2_sum"), i * 4 + (u + 1))
                    act.activation(qkv[:, i * 4 + u, :], cv_w[u % 2], ACT.Silu).then_inc(sem("qkv_silu"), 1)
            for u in range(4):
                done(act, "z2", 0, u)
                act.activation(z_silu[:, u, :], psum[:, u % 2, :], ACT.Silu).then_inc(sem("z_out"), 1)

        def dve_in2(dve):
            dve.wait_ge(sem("dt_added"), 2)
            t, e, g = row_t[0:DNH, :], row_e[0:DNH, :], row_g[0:DNH, :]
            dve.wait_ge(sem("row_ln"), 1)
            dve.scalar_tensor_tensor(g, t, 0.0, e, ALU.max, ALU.add)
            dve.drain()
            dve.tensor_scalar(g, g, head_par[0:DNH, 0:1], -1.0, ALU.mult, ALU.mult)
            dve.drain()
            dve.tensor_tensor_scan(row_c[0:DNH, :], const("restart")[0:DNH, :], g, 0.0, ALU.mult, ALU.add)
            dve.drain()
            dve.sem_inc(sem("row_sums"), 1)
            for gi in range(4):
                done(dve, "pool2", 0, gi)
                if gi >= 2:
                    scale_pool(dve, gi - 2)
                dve.tensor_copy(p_u, psum[:, gi % 2, :])
                dve.drain()
                src = p_u
                for r in range(gi + 1):
                    d = 1 << r
                    dst = p_s[r % 2]
                    dve.tensor_copy(dst[:, 0:d], src[:, 0:d])
                    dve.tensor_tensor(dst[:, d:S], src[:, d:S], src[:, 0:S - d], ALU.add)
                    dve.drain()
                    src = dst
                dve.tensor_tensor(src, src, counts[:, gi, :], ALU.mult)
                dve.drain()
                dve.tensor_tensor(p_mix[gi], src, p_u, ALU.subtract)
                dve.drain()
                dve.sem_inc(sem("pooled"), 1)
            with dve.Fori(0, 3) as i:
                for u in range(4):
                    dve.wait_ge(sem("qkv_out"), i * 4 + (u + 3))
                    x = cv_x[u % 2]

                    def tap(j):
                        return vec2[:, CONV2:CONV2 + 48].rearrange("p (t i u) -> p t i u", t=4, u=4)[:, j, i, u:u + 1]
                    y = cv_w[u % 2]
                    dve.wait_ge(sem("qkv_silu"), i * 4 + (u + 1))
                    dve.tensor_scalar(y, x, tap(3), None, ALU.mult)
                    for j in (2, 1, 0):
                        d = 3 - j
                        dve.drain()
                        dve.scalar_tensor_tensor(y[:, d:S], x[:, 0:S - d], tap(j), y[:, d:S], ALU.mult, ALU.add)
                    dve.drain()
                    dve.sem_inc(sem("conv2_sum"), 1)
            scale_pool(dve, 2)
            scale_pool(dve, 3)
            dve.wait_ge(sem("qkv_silu"), 14)
            dve.wait_ge(sem("z_out"), 4)
            dve.drain()
            dve.sem_inc(sem("in2_done"), 1)

        def scale_pool(dve, g):
            dve.wait_ge(sem("pool_mixed"), g + 1)
            dve.tensor_scalar(ydT[:, g, :], psum[:, 4 + g % 2, :], vec2[:, PSC + g:PSC + g + 1], None, ALU.mult)\
               .then_inc(sem("pool_out"), 1)

        HTN = DNH * LT
        NB = HTN * P
        main = Carve(arena, DN_LO, UNIT_LO)
        d_gc = Carve(arena, HT_LO + 4096, HT_LO + 6144).take(HTN, P)
        d_b, d_c = (Carve(arena, HT_LO - 4096 + NB * m, HT_LO).take(HTN, P) for m in range(2))
        d_kb, d_kd = (Carve(arena, BT_LO + NB * m, BT_LO + 4096).take(HTN, P) for m in range(2))
        d_vb, d_t, d_u, d_y = (main.take(HTN, P) for _ in range(4))
        l2_sq = [main.take(S) for _ in range(2)]
        l2_rt = [main.take(S) for _ in range(2)]
        d_vn = [ap.rearrange("p (h e) -> p h e", h=DNH) for ap in l2_sq]
        d_cols = row_t[:, 0:2 * HTN].rearrange("p (m h t) -> p m h t", m=2, h=DNH)
        d_f = row_t[:, 2 * HTN:7 * HTN].rearrange("p (f m) -> p f m", f=5)
        bcol = d_cols[:, 0].rearrange("p h t -> p (h t)")
        gcol = d_cols[:, 1].rearrange("p h t -> p (h t)")
        qk_heads = qkv

        def head(ap, h):
            return ap[:, h * LT:(h + 1) * LT, :]

        def flat(ap):
            return ap.rearrange("p a b -> p (a b)")

        def tiles(bank):
            return psum[:, bank, :].rearrange("p (t x) -> p t x", t=LT)

        def pe_dn(pe):
            pe.wait_ge(sem("in2_done"), 1)
            for h in range(DNH):
                mm = pe.matmul(psum[:, 2 + h, :], const("row_of").rearrange("p (r x) -> p r x", r=8)[0:DNH, h, :],
                               row_c[0:DNH, :], start=True, stop=True)
            mm.then_inc(sem("spread"), 1)
            for m, row in enumerate((row_b, row_c)):
                for t in range(LT):
                    mm = pe.transpose(psum[:, 6, (m * LT + t) * DNH:(m * LT + t + 1) * DNH],
                                      row[0:DNH, t * P:(t + 1) * P], ident[0:DNH, 0:DNH])
            mm.then_inc(sem("columns"), 1)
            for m in range(8):
                pe.wait_ge(sem("l2_squares"), m + 1)
                if m >= 2:
                    pe.wait_ge(sem("l2_root"), m - 1)
                pe.matmul(psum[:, m % 2, :], ones, l2_sq[m % 2], start=True, stop=True).then_inc(sem("l2_sum"), 1)
            pe.wait_ge(sem("l2_done"), 8)
            pe.wait_ge(sem("spread_out"), 2)
            for h in range(DNH):
                for src, b in ((4 + h, h), (h, 4 + h)):
                    for t in range(LT):
                        c = slice(t * P, (t + 1) * P)
                        mm = pe.matmul(psum[:, b, c], qkv[:, 4 + h, c], qkv[:, src, c], start=True, stop=True)
                mm.then_inc(sem("gram"), 1)
            for h in range(DNH):
                pe.wait_ge(sem("gram_out"), h + 1)
                for src, b in ((4 + h, h), (8 + h, 4 + h)):
                    for t in range(LT):
                        c = slice(t * P, (t + 1) * P)
                        mm = pe.transpose(psum[:, b, c], qkv[:, src, c], ident)
                mm.then_inc(sem("kv_turned"), 1)
            pe.wait_ge(sem("kv_out"), DNH)
            with pe.Fori(0, LEVELS) as l:
                pe.wait_ge(sem("level_mask"), l + 1)
                for h in range(DNH):
                    pe.wait_ge(sem("inverse"), l * DNH + (h + 1))
                    for t in range(LT):
                        m = h * LT + t
                        mm = pe.matmul(psum[:, h, t * P:(t + 1) * P], d_gc[:, m, :], d_u[:, m, :], start=True, stop=True)
                    mm.then_inc(sem("left"), 1)
                for h in range(DNH):
                    pe.wait_ge(sem("left_out"), l * DNH + (h + 1))
                    for t in range(LT):
                        m = h * LT + t
                        c = slice(t * P, (t + 1) * P)
                        pe.matmul(psum[:, h, c], d_y[:, m, :], d_t[:, m, :], start=True, stop=True)
                        mm = pe.matmul(psum[:, 4 + h, c], d_t[:, m, :], d_y[:, m, :], start=True, stop=True)
                    mm.then_inc(sem("both"), 1)
            pe.wait_ge(sem("inverse"), (LEVELS + 1) * DNH)
            for h in range(DNH):
                for t in range(LT):
                    m = h * LT + t
                    mm = pe.matmul(psum[:, h, t * P:(t + 1) * P], d_kb[:, m, :], d_u[:, m, :], start=True, stop=True)
                mm.then_inc(sem("w"), 1)
            pe.wait_ge(sem("w_out2"), DNH)
            pe.wait_ge(sem("q_decayed"), 1)
            for t in range(LT):
                if t:
                    pe.wait_ge(sem("dn_state"), t)
                for h in range(DNH):
                    m = h * LT + t
                    c = slice(h * P, (h + 1) * P)
                    mm = pe.matmul(psum[:, 0, c], d_u[:, m, :], d_vb[:, m, :], start=True, stop=(t == 0))
                    if t:
                        mm = pe.matmul(psum[:, 0, c], d_gc[:, m, :], d_s2[(t - 1) % 2][:, h, :], start=False, stop=True)
                mm.then_inc(sem("new_values"), 1)
                pe.wait_ge(sem("new_values_out"), t + 1)
                if t < LT - 1:
                    for h in range(DNH):
                        mm = pe.matmul(psum[:, 2, h * P:(h + 1) * P], d_kd[:, h * LT + t, :], d_vn[t % 2][:, h, :],
                                       start=True, stop=True)
                    mm.then_inc(sem("state_sum"), 1)
                if t:
                    pe.wait_ge(sem("dn_out"), t)
                for h in range(DNH):
                    m = h * LT + t
                    c = slice(h * P, (h + 1) * P)
                    if t:
                        pe.matmul(psum[:, 1, c], d_s2[(t - 1) % 2][:, h, :], qkv[:, h, t * P:(t + 1) * P], start=True, stop=False)
                    mm = pe.matmul(psum[:, 1, c], d_vn[t % 2][:, h, :], d_b[:, m, :], start=(t == 0), stop=True)
                mm.then_inc(sem("dn_sums"), 1)
            for h in range(DNH):
                pe.wait_ge(sem("dn_squares"), 1)
                mm = pe.matmul(psum[:, 4 + h, :], ones, flat(head(d_c, h)), start=True, stop=True)
            mm.then_inc(sem("dn_mean"), 1)

        def act_dn(act):
            act.wait_ge(sem("in2_done"), 1)
            act.wait_ge(sem("spread"), 1)
            act.activation(d_gc.rearrange("p (h t) x -> p h (t x)", h=DNH), psum[:, 2:6, :], ACT.Copy).then_inc(sem("spread_out"), 1)
            for m in range(8):
                if m >= 2:
                    act.wait_ge(sem("l2_sum"), m - 1)
                act.activation(l2_sq[m % 2], qkv[:, m, :], ACT.Square).then_inc(sem("l2_squares"), 1)
                if m >= 1:
                    l2_root(act, m - 1)
            l2_root(act, 7)
            act.wait_ge(sem("d_factors"), 1)
            act.activation(d_f[:, 4, :], gcol, ACT.Exp)
            act.activation(d_f[:, 2, :], d_f[:, 3, :], ACT.Exp)
            act.activation(d_f[:, 1, :], d_f[:, 1, :], ACT.Exp).then_inc(sem("d_exps"), 1)
            act.wait_ge(sem("differences"), 1)
            act.activation(flat(d_b), flat(d_b), ACT.Exp)
            act.activation(flat(d_c), flat(d_c), ACT.Exp, scale=-1.0).then_inc(sem("decays"), 1)
            act.activation(flat(d_y), flat(d_gc), ACT.Exp).then_inc(sem("row_exp"), 1)
            with act.Fori(0, LEVELS) as l:
                for h in range(DNH):
                    act.wait_ge(sem("left"), l * DNH + (h + 1))
                    if h == 0:
                        act.wait_ge(sem("y_free"), l + 1)
                    act.activation(head(d_y, h), tiles(h), ACT.Copy).then_inc(sem("left_out"), 1)
            for h in range(DNH):
                act.wait_ge(sem("w"), h + 1)
                act.activation(head(d_gc, h), tiles(h), ACT.Copy, scale=-1.0).then_inc(sem("w_out2"), 1)
            for t in range(LT):
                act.wait_ge(sem("dn_sums"), t + 1)
                act.activation(d_y.rearrange("p (h t) x -> p h t x", h=DNH)[:, :, t, :],
                               psum[:, 1, :].rearrange("p (h x) -> p h x", h=DNH), ACT.Copy).then_inc(sem("dn_out"), 1)
            act.drain()
            act.activation(flat(d_c), flat(d_y), ACT.Square).then_inc(sem("dn_squares"), 1)
            act.wait_ge(sem("dn_mean"), 1)
            act.activation(d_b.rearrange("p (h t) x -> p h (t x)", h=DNH), psum[:, 4:8, :], ACT.Sqrt, bias=eps, scale=1.0 / P)\
               .then_inc(sem("dn_root"), 1)

        def l2_root(act, m):
            act.wait_ge(sem("l2_sum"), m + 1)
            if m >= 2:
                act.wait_ge(sem("l2_done"), m - 1)
            act.activation(l2_rt[m % 2], psum[:, m % 2, :], ACT.Sqrt, bias=eps).then_inc(sem("l2_root"), 1)

        def dve_dn(dve):
            dve.wait_ge(sem("columns"), 1)
            dve.tensor_copy(d_cols.rearrange("p m h t -> p m t h"),
                            psum[:, 6, 0:2 * HTN].rearrange("p (m t h) -> p m t h", m=2, t=LT)).then_inc(sem("spread_out"), 1)
            dve.wait_ge(sem("spread_out"), 2)
            dve.tensor_copy(d_f[:, 3, :], d_gc[:, :, P - 1])
            dve.drain()
            dve.tensor_tensor(d_f[:, 1, :], d_f[:, 3, :], gcol, ALU.subtract)
            dve.drain()
            dve.sem_inc(sem("d_factors"), 1)
            dve.tensor_tensor(d_b, d_gc, bcast(gcol, P), ALU.subtract)
            dve.drain()
            off = bmid(const("off_diagonal"), HTN)
            dve.scalar_tensor_tensor(d_c, d_b, 0.0, off, ALU.max, ALU.mult)
            dve.drain()
            dve.scalar_tensor_tensor(d_b, d_b, 0.0, off, ALU.min, ALU.mult)
            dve.drain()
            dve.sem_inc(sem("differences"), 1)
            for m in range(8):
                dve.wait_ge(sem("l2_root"), m + 1)
                dve.reciprocal(l2_rt[m % 2], l2_rt[m % 2])
                dve.drain()
                dve.scalar_tensor_tensor(qkv[:, m, :], qkv[:, m, :], P ** -0.5 if m < 4 else 1.0, l2_rt[m % 2], ALU.mult, ALU.mult)\
                   .then_inc(sem("l2_done"), 1)
            dve.wait_ge(sem("decays"), 1)
            dve.tensor_tensor(d_b, d_b, bmid(const("upper"), HTN), ALU.mult)
            dve.tensor_tensor(d_c, d_c, bmid(const("lower_strict"), HTN), ALU.mult)
            dve.tensor_tensor(d_f[:, 0, :], d_f[:, 4, :], bcol, ALU.mult)
            dve.drain()
            for h in range(DNH):
                dve.wait_ge(sem("gram"), h + 1)
                dve.tensor_tensor(head(d_c, h), head(d_c, h), tiles(h), ALU.mult)
                dve.tensor_tensor(head(d_b, h), head(d_b, h), tiles(4 + h), ALU.mult)
                dve.drain()
                dve.sem_inc(sem("gram_out"), 1)
            dve.tensor_tensor(d_c, d_c, bcast(bcol, P), ALU.mult)
            idm = bmid(ident, HTN)
            dve.tensor_copy(d_t, idm)
            dve.tensor_copy(d_u, idm)
            for h in range(DNH):
                dve.wait_ge(sem("kv_turned"), h + 1)
                hs = slice(h * LT, (h + 1) * LT)
                dve.tensor_tensor(head(d_kb, h), tiles(h), bcast(d_f[:, 0, hs], P), ALU.mult)
                dve.tensor_tensor(head(d_kd, h), tiles(h), bcast(d_f[:, 1, hs], P), ALU.mult)
                dve.tensor_tensor(head(d_vb, h), tiles(4 + h), bcast(bcol[:, hs], P), ALU.mult)
                dve.drain()
                dve.sem_inc(sem("kv_out"), 1)
            dve.wait_ge(sem("row_exp"), 1)
            dve.tensor_tensor(flat(qkv[:, 0:4, :]), flat(qkv[:, 0:4, :]), flat(d_y), ALU.mult)
            dve.drain()
            dve.sem_inc(sem("q_decayed"), 1)
            dve.sem_inc(sem("inverse"), DNH)
            with dve.Fori(0, LEVELS) as l:
                dve.tensor_tensor(d_gc, d_c, masks[:, bass.ds(l + 1, 1), :].to_broadcast([P, HTN, P]), ALU.mult)
                dve.drain()
                dve.sem_inc(sem("level_mask"), 1)
                dve.sem_inc(sem("y_free"), 1)
                for h in range(DNH):
                    dve.wait_ge(sem("both"), l * DNH + (h + 1))
                    dve.tensor_tensor(head(d_t, h), head(d_t, h), tiles(h), ALU.subtract)
                    dve.tensor_tensor(head(d_u, h), head(d_u, h), tiles(4 + h), ALU.subtract)
                    dve.drain()
                    dve.sem_inc(sem("inverse"), 1)
            for t in range(LT):
                dve.wait_ge(sem("new_values"), t + 1)
                dve.tensor_copy(d_vn[t % 2], psum[:, 0, :].rearrange("p (h e) -> p h e", h=DNH)).then_inc(sem("new_values_out"), 1)
                if t == LT - 1:
                    continue
                gl = d_f[:, 2, :].rearrange("p (h t) -> p h t", h=DNH)[:, :, t]
                dve.wait_ge(sem("state_sum"), t + 1)
                ss = psum[:, 2, :].rearrange("p (h e) -> p h e", h=DNH)
                if t == 0:
                    dve.tensor_copy(d_s2[0], ss)
                else:
                    dve.tensor_tensor(d_s2[t % 2], d_s2[(t - 1) % 2], bcast(gl, P), ALU.mult)
                    dve.drain()
                    dve.tensor_tensor(d_s2[t % 2], d_s2[t % 2], ss, ALU.add)
                dve.drain()
                dve.sem_inc(sem("dn_state"), 1)
            dve.wait_ge(sem("dn_root"), 1)
            dve.reciprocal(flat(d_b), flat(d_b))
            dve.drain()
            dve.tensor_tensor(d_y, d_y, d_b, ALU.mult)
            dve.drain()
            dve.scalar_tensor_tensor(flat(ydT[:, 4:8, :]), flat(d_y), vec1[:, DNN:DNN + 1], flat(z_silu), ALU.mult, ALU.mult)
            dve.drain()
            dve.sem_inc(sem("dn_done"), 1)

        d_s2 = [ap.rearrange("p (h e) -> p h e", h=DNH) for ap in l2_rt]

        def add_plain(dve, c, bank):
            return dve.tensor_tensor(X2[:, c, :], bank, X2[:, c, :], ALU.add)

        w_out2 = cut(A["w_out_2"][0], P)
        pe_wout2, dve_wout2 = residual("w_out2nd", 2, [((lambda i, u=u: w_out2[i * 4 + u]),) + unit_place(4 + u) for u in range(4)],
                                       ydT, add_plain, (("dn_done", 1),), [4, 5, 6, 7])

        hx = Carve(arena, BT_LO, BT_LO + 4096).take(KC, S)
        spare = Carve(arena, HT_LO + 4096, HT_LO + 6144)
        work2 = spare.take(S)
        work3 = spare.take(S)
        n_x = norm(X2, hx, S, lambda k: vec2[:, XN + k:XN + k + 1], None, 4, work2, before=(("w_out2nd_done", 1),))
        xr = Carve(arena, CT_LO, UNIT_LO)
        mem_tok = xr.take(CT_, D)
        mem_raw = xr.take(KC, C)
        memT = xr.take(KC, C)
        x_q = xr.take(KC, S)
        x_k = xr.take(KC, C)
        x_v = xr.take(CT_, D)
        x_prob = [xr.take(C) for _ in range(2)]
        x_pt = [xr.take(CT_, S) for _ in range(2)]
        x_st = xr.take(4, 2)
        xoT = Carve(arena, CT_LO - 4096, CT_LO).take(KC, S)
        n_mem = norm(mem_raw, memT, C, lambda k: vec2[:, MEMN + k:MEMN + k + 1], None, 5, work3, before=(("mem_out", KC),))
        w_xq, w_xk, w_xo = (cut(A[n][0], P) for n in ("w_xq_2", "w_xk_2", "w_xo_2"))
        w_xv = cut(A["w_xv_2"][0], P)
        for name, w in (("xk", w_xk), ("xv", w_xv), ("xq", w_xq)):
            ws.phase(name, 1, [((lambda i, u=u, w=w: w[u]),) + unit_place(u) for u in range(8)])
        XSCALE = 256 ** -0.5

        def sp_mem(sp):
            sp.wait_ge(sem("w_out2nd_done"), 1)
            sp.dma_start(mem_tok, A["mem_2"][0].rearrange("(t p) d -> p t d", p=P)).then_inc(sem("mem_in"), 16)

        def pe_mem(pe):
            pe.wait_ge(sem("mem_in"), 16)
            for k in range(KC):
                if k >= 2:
                    pe.wait_ge(sem("mem_out"), k - 1)
                for t in range(CT_):
                    mm = pe.transpose(psum[:, 6 + k % 2, t * P:(t + 1) * P], mem_tok[:, t, k * P:(k + 1) * P], ident)
                mm.then_inc(sem("mem_turned"), 1)

        def dve_mem(dve):
            for k in range(KC):
                dve.wait_ge(sem("mem_turned"), k + 1)
                dve.tensor_copy(mem_raw[:, k, :], psum[:, 6 + k % 2, 0:C]).then_inc(sem("mem_out"), 1)

        def pe_xproj(pe):
            pe.wait_ge(sem("normed"), n_mem + 1)
            n = 0
            for u in range(8):
                if n >= 2:
                    pe.wait_ge(sem("xproj_out"), n - 1)
                product(pe, "xk", 0, u, memT, n % 2, C)
                n += 1
            for u in range(8):
                pe.wait_ge(sem("xproj_out"), n - 1)
                ws.arrived(pe, "xv", 0, u)
                for t in range(CT_):
                    for k in range(KC):
                        mm = pe.matmul(psum[:, n % 2, t * P:(t + 1) * P], memT[:, k, t * P:(t + 1) * P],
                                       ws.dst("xv", u)[:, k, :], start=(k == 0), stop=(k == KC - 1))
                mm.then_inc(sem("weights_used"), 1)
                n += 1
            for u in range(8):
                pe.wait_ge(sem("xproj_out"), n - 1)
                product(pe, "xq", 0, u, hx, n % 2)
                n += 1

        def act_xproj(act):
            n = 0
            for name, dst in (("xk", lambda u: x_k[:, u, :]), ("xv", lambda u: x_v[:, :, u * P:(u + 1) * P]), ("xq", lambda u: x_q[:, u, :])):
                for u in range(8):
                    done(act, name, 0, u)
                    src = psum[:, n % 2, 0:S if name == "xq" else C]
                    if name == "xv":
                        src = src.rearrange("p (t n) -> p t n", t=CT_)
                    act.activation(dst(u), src, ACT.Copy).then_inc(sem("xproj_out"), 1)
                    n += 1

        def pe_xattn(pe):
            pe.wait_ge(sem("xproj_out"), 24)
            for s in range(18):
                if s < 16:
                    j, t = s // 4, s % 4
                    if s >= 2:
                        pe.wait_ge(sem("x_exps"), s - 1)
                    for c in range(2):
                        mm = pe.matmul(psum[:, 2 + s % 2, 0:C], x_q[:, 2 * j + c, t * P:(t + 1) * P], x_k[:, 2 * j + c, :],
                                       start=(c == 0), stop=(c == 1))
                    mm.then_inc(sem("x_scores"), 1)
                if s >= 2:
                    r = s - 2
                    pe.wait_ge(sem("x_probs"), r + 1)
                    if r >= 2:
                        pe.wait_ge(sem("x_turned_out"), r - 1)
                    for m in range(CT_):
                        mm = pe.transpose(psum[:, 4 + r % 2, m * P:(m + 1) * P], x_prob[r % 2][:, m * P:(m + 1) * P], ident)
                    mm.then_inc(sem("x_turned"), 1)
                if s >= 6 and (s - 6) % 4 == 0:
                    pe_xvalues(pe, (s - 6) // 4)
            pe_xvalues(pe, 3)

        def pe_xvalues(pe, j):
            pe.wait_ge(sem("x_turned_out"), 4 * j + 4)
            for c in range(2):
                if j:
                    pe.wait_ge(sem("x_attended"), 2 * j - 1 + c)
                for m in range(CT_):
                    mm = pe.matmul(psum[:, 6 + c, :], x_v[:, m, (2 * j + c) * P:(2 * j + c + 1) * P], x_pt[j % 2][:, m, :],
                                   start=(m == 0), stop=(m == CT_ - 1))
                mm.then_inc(sem("x_weighted"), 1)

        def act_xattn(act):
            for s in range(18):
                if s < 16:
                    act.wait_ge(sem("x_max"), s + 1)
                    if s >= 2:
                        act.wait_ge(sem("x_turned"), s - 1)
                    act.activation(x_prob[s % 2], psum[:, 2 + s % 2, 0:C], ACT.Exp, bias=x_st[:, s % 2, 1:2], scale=XSCALE,
                                   accum_out=x_st[:, 2 + s % 2, 0:1]).then_inc(sem("x_exps"), 1)
                if s >= 2:
                    r = s - 2
                    j, t = r // 4, r % 4
                    act.wait_ge(sem("x_turned"), r + 1)
                    if t == 0 and j >= 2:
                        act.wait_ge(sem("x_weighted"), 2 * (j - 1))
                    act.activation(x_pt[j % 2][:, :, t * P:(t + 1) * P], psum[:, 4 + r % 2, 0:C].rearrange("p (m n) -> p m n", m=CT_),
                                   ACT.Copy).then_inc(sem("x_turned_out"), 1)
                if s >= 6 and (s - 6) % 4 == 0:
                    act_xvalues(act, (s - 6) // 4)
            act_xvalues(act, 3)

        def act_xvalues(act, j):
            for c in range(2):
                act.wait_ge(sem("x_weighted"), 2 * j + c + 1)
                act.activation(xoT[:, 2 * j + c, :], psum[:, 6 + c, :], ACT.Copy).then_inc(sem("x_attended"), 1)

        def dve_xattn(dve):
            for s in range(17):
                if s < 16:
                    dve.wait_ge(sem("x_scores"), s + 1)
                    dve.tensor_reduce(x_st[:, s % 2, 0:1], psum[:, 2 + s % 2, 0:C], AX, ALU.max)
                    dve.drain()
                    dve.tensor_scalar(x_st[:, s % 2, 1:2], x_st[:, s % 2, 0:1], -XSCALE, None, ALU.mult).then_inc(sem("x_max"), 1)
                if s >= 1:
                    r = s - 1
                    dve.wait_ge(sem("x_exps"), r + 1)
                    dve.reciprocal(x_st[:, 2 + r % 2, 1:2], x_st[:, 2 + r % 2, 0:1])
                    dve.drain()
                    dve.tensor_scalar(x_prob[r % 2], x_prob[r % 2], x_st[:, 2 + r % 2, 1:2], None, ALU.mult).then_inc(sem("x_probs"), 1)

        pe_xo, dve_xo = residual("xo", 2, [((lambda i, u=u: w_xo[i * 4 + u]),) + unit_place(u) for u in range(4)],
                                 xoT, add_plain, (("x_attended", 8),))

        n_mlp = norm(X2, hx, S, lambda k: vec2[:, MLPN + k:MLPN + k + 1], None, 4, work2, before=(("xo_done", 1),))
        FF = 4 * D
        w_up2 = cut(A["w_up_2"][0], P)
        ws.phase("up", 4, [((lambda i, u=u: w_up2[i * 8 + u]),) + unit_place(u) for u in range(8)])
        w_dn2 = A["w_down_2"][0].rearrange("(b k p) (i c n) -> i c b p k n", b=4, p=P, c=2, n=P)
        ws.phase("down", 4, [((lambda i, c=c, b=b: w_dn2[i, c, b]),) + unit_place(4 * c + b)
                             for c in range(2) for b in range(4)])
        act2 = Carve(arena, CT_LO - 4096, RING_LO).take(FF // P, S)

        def pe_mlp(pe):
            pe.wait_ge(sem("normed"), n_mlp + 1)
            with pe.Fori(0, 4) as i:
                for u in range(8):
                    pe.wait_ge(sem("relu"), i * 8 + (u + 1))
                    product(pe, "up", i, u, hx, u % 4)
            pe.wait_ge(sem("squared"), FF // P)
            with pe.Fori(0, 4) as i:
                for c in range(2):
                    pe.wait_ge(sem("down_out"), i * 2 + (c + 1))
                    for b in range(4):
                        ws.arrived(pe, "down", i, 4 * c + b)
                        for k in range(KC):
                            mm = pe.matmul(psum[:, 4 + c, :], ws.dst("down", 4 * c + b)[:, k, :], act2[:, b * KC + k, :],
                                           start=(b == 0 and k == 0), stop=(b == 3 and k == KC - 1))
                        mm.then_inc(sem("weights_used"), 1)

        def act_mlp(act):
            act.sem_inc(sem("relu"), 4)
            act.wait_ge(sem("xo_done"), 1)
            with act.Fori(0, 4) as i:
                for u in range(8):
                    done(act, "up", i, u)
                    act.activation(act2[:, i * 8 + u, :], psum[:, u % 4, :], ACT.Relu).then_inc(sem("relu"), 1)

        def dve_mlp(dve):
            dve.sem_inc(sem("down_out"), 2)
            with dve.Fori(0, 4) as i:
                for u in range(8):
                    dve.wait_ge(sem("relu"), i * 8 + (u + 5))
                    a = act2[:, i * 8 + u, :]
                    dve.tensor_tensor(a, a, a, ALU.mult).then_inc(sem("squared"), 1)
            with dve.Fori(0, 4) as i:
                for c in range(2):
                    done(dve, "down", i, 4 * c + 3)
                    dve.tensor_tensor(X2[:, i * 2 + c, :], psum[:, 4 + c, :], X2[:, i * 2 + c, :], ALU.add)\
                       .then_inc(sem("down_out"), 1)
            dve.drain()
            dve.sem_inc(sem("mlp_done"), 1)

        n_last = norm(X2, hx, S, lambda k: vec2[:, FIN2 + k:FIN2 + k + 1], None, 4, work2, before=(("mlp_done", 1),))
        out_tok = Carve(arena, CT_LO, CT_LO + 4096).take(LT, D)

        def pe_last(pe):
            pe.wait_ge(sem("normed"), n_last + 1)
            for n in range(8):
                if n >= 4:
                    pe.wait_ge(sem(f"last_out_{n % 2}"), (n - 2) // 2)
                for c in range(4):
                    mm = pe.transpose(psum[:, n % 4, c * P:(c + 1) * P], hx[:, 4 * (n % 2) + c, (n // 2) * P:(n // 2 + 1) * P], ident)
                mm.then_inc(sem("last_turned"), 1)

        def last_copy(eng, n):
            eng.wait_ge(sem("last_turned"), n + 1)
            dst, src = out_tok[:, n // 2, (n % 2) * 512:(n % 2) * 512 + 512], psum[:, n % 4, :]
            ins = eng.activation(dst, src, ACT.Copy) if n % 2 else eng.tensor_copy(dst, src)
            ins.then_inc(sem(f"last_out_{n % 2}"), 1)

        def act_last(act):
            for n in range(1, 8, 2):
                last_copy(act, n)

        def dve_last(dve):
            for n in range(0, 8, 2):
                last_copy(dve, n)

        def sp_last(sp):
            for t in range(LT):
                for half in range(2):
                    sp.wait_ge(sem(f"last_out_{half}"), t + 1)
                sp.dma_start(out[0].rearrange("(t p) d -> t p d", p=P)[t], out_tok[:, t, :]).then_inc(sem("stored"), 16)
            sp.wait_ge(sem("stored"), 16 * LT)

        def N(f, m):
            return lambda e: f(e, m)
        PE_STEPS = [pe_setup, pe_mod, N(pe_norm, n_ctx), N(pe_norm, n_lat), pe_hg, pe_attn, pe_merge, pe_wout, N(pe_norm, n_ffn), pe_router, pe_gather, pe_experts, pe_scatter, N(pe_norm, n_fin1), N(pe_norm, n_mix), pe_in2, pe_dn, pe_wout2, N(pe_norm, n_x), pe_mem, N(pe_norm, n_mem), pe_xproj, pe_xattn, pe_xo, N(pe_norm, n_mlp), pe_mlp, N(pe_norm, n_last), pe_last]
        DVE_STEPS = [dve_setup, dve_mod, dve_gains, N(dve_norm, n_ctx), N(dve_norm, n_lat), dve_hg, dve_attn, dve_merge, dve_wout, N(dve_norm, n_ffn), dve_router, dve_gather, dve_experts, dve_scatter, N(dve_norm, n_fin1), N(dve_norm, n_mix), dve_in2, dve_dn, dve_wout2, N(dve_norm, n_x), dve_mem, N(dve_norm, n_mem), dve_xattn, dve_xo, N(dve_norm, n_mlp), dve_mlp, N(dve_norm, n_last), dve_last]
        ACT_STEPS = [act_setup, act_mod, N(act_norm, n_ctx), N(act_norm, n_lat), act_hg, act_attn, act_merge, N(act_norm, n_ffn), act_router, act_gather, act_experts, N(act_norm, n_fin1), N(act_norm, n_mix), act_in2, act_dn, N(act_norm, n_x), N(act_norm, n_mem), act_xproj, act_xattn, N(act_norm, n_mlp), act_mlp, N(act_norm, n_last), act_last]
        SP_STEPS = [sp_setup] + [lambda e, n=n: ws.load(e, n) for n in ws.phases]
        SP_STEPS.insert(6, sp_router)
        SP_STEPS.insert(1 + 1 + 1 + list(ws.phases).index('pool2'), sp_small2)
        SP_STEPS.insert(SP_STEPS.index(sp_small2) + 5, sp_mem)
        SP_STEPS.append(sp_last)
        POOL_STEPS = []

        block = ctx.enter_context(nc.Block())

        @block.sync
        def _(sp):
            for step in SP_STEPS:
                step(sp)

        @block.tensor
        def _(pe):
            for step in PE_STEPS:
                step(pe)

        @block.vector
        def _(dve):
            for step in DVE_STEPS:
                step(dve)

        @block.scalar
        def _(act):
            for step in ACT_STEPS:
                step(act)

        @block.gpsimd
        def _(pool):
            for step in POOL_STEPS:
                step(pool)


_INS = ["x", "c", "ctx", "c_ctx", "ada_w", "ada_b", "norm1_g", "norm2_g", "w_in", "hg_lb_logits", "hg_norm_g", "conv_w",
        "q_norm_g", "k_norm_g", "w_proj_a", "w_proj_b", "w_proj_c", "w_out", "router_w", "w_gate", "w_up", "w_down",
        "final_norm_g", "mem_2", "norm_mix_g_2", "w_in_2", "w_pool_2", "pool_scale_2", "conv_w_2", "a_log_2",
        "dt_bias_2", "dn_out_norm_g_2", "w_out_2", "norm_xattn_g_2", "mem_norm_g_2", "w_xq_2", "w_xk_2", "w_xv_2",
        "w_xo_2", "norm_mlp_g_2", "w_up_2", "w_down_2", "final_norm_g_2"]


def kernel(**inputs):
    import concourse.bacc as _bacc
    from concourse.bass_utils import run_bass_kernel_spmd as _run

    nc = _bacc.Bacc("TRN2", target_bir_lowering=False, num_devices=1)
    arrays, args = {}, {}
    for name in _INS:
        a = np.ascontiguousarray(inputs[name])
        arrays[f"in_{name}"] = a
        args[name] = nc.dram_tensor(f"in_{name}", a.shape, mybir.dt.from_np(a.dtype), kind="ExternalInput").ap()
    arrays["const_table"] = CONST
    args["const_table"] = nc.dram_tensor("const_table", CONST.shape, F32, kind="ExternalInput").ap()
    out = nc.dram_tensor("out", (1, S, D), F32, kind="ExternalOutput").ap()
    mixed_block_kernel(nc, args, out)
    r = _run(nc, [arrays], core_ids=[0])
    return r.results[0]["out"]
```
